# Optimizing a Trainium2 kernel written in Bass

```python
import math
import jax
import jax.numpy as jnp
from jax import lax
import numpy as np
import jax, jax.numpy as jnp

D_MODEL = 2048
BATCH = 1
SEQ = 256
DEPTH = 1

MLA_HEADS = 8
QK_NOPE = 128
QK_ROPE = 64
V_HEAD = 128
Q_LORA = 512
KV_LORA = 512
ROPE_THETA = 10000.0
Q_BLOCK = 128
GDN_HEADS = 8
GDN_DK = 128
GDN_DV = 128
CONV_WIDTH = 4
CHUNK = 64
GDN_QK = GDN_HEADS * GDN_DK
GDN_V = GDN_HEADS * GDN_DV
CONV_CH = 2 * GDN_QK + GDN_V
D_FF = ((8 * D_MODEL // 3 + 255) // 256) * 256
EPS = 1e-6
IN_SIZES = (Q_LORA, KV_LORA, QK_ROPE, GDN_QK, GDN_QK, GDN_V, GDN_V, GDN_HEADS, GDN_HEADS, 2 * D_MODEL)
IN_WIDTH = Q_LORA + KV_LORA + QK_ROPE + 2 * GDN_QK + 2 * GDN_V + 2 * GDN_HEADS + 2 * D_MODEL


def _rmsnorm(x, w):
    xf = x.astype(jnp.float32)
    y = xf * lax.rsqrt(jnp.mean(xf * xf, axis=-1, keepdims=True) + EPS)
    return (y * w.astype(jnp.float32)).astype(x.dtype)

def _split_cols(p):
    outs, off = [], 0
    for n in IN_SIZES:
        outs.append(p[..., off:off + n])
        off += n
    return outs

def _rope_tables(positions):
    inv_freq = 1.0 / (ROPE_THETA ** (jnp.arange(0, QK_ROPE, 2, dtype=jnp.float32) / QK_ROPE))
    ang = positions.astype(jnp.float32)[..., None] * inv_freq
    return jnp.cos(ang), jnp.sin(ang)

def _rope(x, cos, sin):
    xf = x.astype(jnp.float32)
    x1, x2 = jnp.split(xf, 2, axis=-1)
    return jnp.concatenate([x1 * cos - x2 * sin, x2 * cos + x1 * sin], axis=-1).astype(x.dtype)

def _mla_branch(c_q, c_kv, k_pe, q_norm, kv_norm, w_uq, w_ukv, cos, sin):
    B, T, _ = c_q.shape
    q = (_rmsnorm(c_q, q_norm) @ w_uq).reshape(B, T, MLA_HEADS, QK_NOPE + QK_ROPE)
    q_nope, q_pe = q[..., :QK_NOPE], q[..., QK_NOPE:]
    q_pe = _rope(q_pe, cos[:, :, None, :], sin[:, :, None, :])
    kv = (_rmsnorm(c_kv, kv_norm) @ w_ukv).reshape(B, T, MLA_HEADS, QK_NOPE + V_HEAD)
    k_nope, v = kv[..., :QK_NOPE], kv[..., QK_NOPE:]
    k_pe = _rope(k_pe, cos, sin)
    scale = (QK_NOPE + QK_ROPE) ** -0.5
    outs = []
    for i in range(T // Q_BLOCK):
        q0, k_end = i * Q_BLOCK, (i + 1) * Q_BLOCK
        s = (jnp.einsum('bqhd,bkhd->bhqk', q_nope[:, q0:k_end], k_nope[:, :k_end])
             + jnp.einsum('bqhr,bkr->bhqk', q_pe[:, q0:k_end], k_pe[:, :k_end]))
        s = s.astype(jnp.float32) * scale
        mask = jnp.arange(k_end)[None, :] <= (q0 + jnp.arange(Q_BLOCK))[:, None]
        p = jax.nn.softmax(jnp.where(mask, s, -jnp.inf), axis=-1).astype(v.dtype)
        outs.append(jnp.einsum('bhqk,bkhd->bqhd', p, v[:, :k_end]))
    return jnp.concatenate(outs, axis=1).reshape(B, T, MLA_HEADS * V_HEAD)

def _causal_conv_silu(u, w):
    kern = w[:, None, :].astype(u.dtype)
    y = lax.conv_general_dilated(u, kern, window_strides=(1,), padding=[(CONV_WIDTH - 1, 0)],
                                 dimension_numbers=('NWC', 'WIO', 'NWC'),
                                 feature_group_count=u.shape[-1])
    return jax.nn.silu(y)

def _l2norm(x):
    xf = x.astype(jnp.float32)
    return xf * lax.rsqrt(jnp.sum(xf * xf, axis=-1, keepdims=True) + EPS)

def _gated_delta_chunked(q, k, v, beta, g):
    B, T, H, DK = q.shape
    DV = v.shape[-1]
    N = T // CHUNK
    to_chunks = lambda a: a.reshape(B, N, CHUNK, H, -1).transpose(0, 3, 1, 2, 4)
    q, k, v = to_chunks(q), to_chunks(k), to_chunks(v)
    beta = beta.reshape(B, N, CHUNK, H).transpose(0, 3, 1, 2)
    g = g.reshape(B, N, CHUNK, H).transpose(0, 3, 1, 2)
    G = jnp.cumsum(g, axis=-1)
    idx = jnp.arange(CHUNK)
    lower = idx[:, None] >= idx[None, :]
    strict = idx[:, None] > idx[None, :]
    diff = G[..., :, None] - G[..., None, :]
    decay = jnp.where(lower, jnp.exp(jnp.where(lower, diff, 0.0)), 0.0)
    kb = k * beta[..., None]
    Lmat = jnp.where(strict, jnp.einsum('bhncd,bhnsd->bhncs', kb, k) * decay, 0.0)
    A = Lmat + jnp.eye(CHUNK, dtype=jnp.float32)
    rhs = jnp.concatenate([v * beta[..., None], kb * jnp.exp(G)[..., None]], axis=-1)
    sol = lax.linalg.triangular_solve(A, rhs, left_side=True, lower=True, unit_diagonal=True)
    u, w = sol[..., :DV], sol[..., DV:]
    attn = jnp.where(lower, jnp.einsum('bhncd,bhnsd->bhncs', q, k) * decay, 0.0)

    def step(S, inp):
        q_c, k_c, u_c, w_c, G_c, a_c = inp
        v_new = u_c - jnp.einsum('bhcd,bhde->bhce', w_c, S)
        o = (jnp.einsum('bhcd,bhde->bhce', q_c * jnp.exp(G_c)[..., None], S)
             + jnp.einsum('bhcs,bhse->bhce', a_c, v_new))
        G_last = G_c[..., -1]
        k_dec = k_c * jnp.exp(G_last[..., None] - G_c)[..., None]
        S = S * jnp.exp(G_last)[..., None, None] + jnp.einsum('bhcd,bhce->bhde', k_dec, v_new)
        return S, o

    xs = tuple(jnp.moveaxis(a, 2, 0) for a in (q, k, u, w, G, attn))
    S0 = jnp.zeros((B, H, DK, DV), jnp.float32)
    _, o = lax.scan(step, S0, xs)
    return o.transpose(1, 0, 3, 2, 4).reshape(B, T, H, DV)

def _gdn_branch(qkv, z, b_logit, a_logit, conv_w, A_log, dt_bias, gdn_norm):
    B, T, _ = qkv.shape
    dtype = qkv.dtype
    qkv = _causal_conv_silu(qkv, conv_w)
    q = _l2norm(qkv[..., :GDN_QK].reshape(B, T, GDN_HEADS, GDN_DK)) * (GDN_DK ** -0.5)
    k = _l2norm(qkv[..., GDN_QK:2 * GDN_QK].reshape(B, T, GDN_HEADS, GDN_DK))
    v = qkv[..., 2 * GDN_QK:].reshape(B, T, GDN_HEADS, GDN_DV).astype(jnp.float32)
    beta = jax.nn.sigmoid(b_logit.astype(jnp.float32))
    g = -jnp.exp(A_log.astype(jnp.float32)) * jax.nn.softplus(a_logit.astype(jnp.float32) + dt_bias.astype(jnp.float32))
    o = _gated_delta_chunked(q, k, v, beta, g)
    o = o * lax.rsqrt(jnp.mean(o * o, axis=-1, keepdims=True) + EPS) * gdn_norm.astype(jnp.float32)
    o = o * jax.nn.silu(z.reshape(B, T, GDN_HEADS, GDN_DV).astype(jnp.float32))
    return o.reshape(B, T, GDN_V).astype(dtype)

def first_inputs(seed: int = 0) -> dict:
    key = jax.random.key(seed)
    ks = jax.random.split(key, 24)
    L, D = DEPTH, D_MODEL
    f32 = jnp.float32

    def nrm(k, shape, fan_in, gain=1.0):
        return gain * fan_in ** -0.5 * jax.random.normal(k, shape, f32)

    def gain(k, shape):
        return 1.0 + 0.02 * jax.random.normal(k, shape, f32)

    x = jax.random.normal(ks[0], (BATCH, SEQ, D), f32)
    c = jax.random.normal(ks[1], (BATCH, D), f32)
    positions = (jnp.arange(SEQ, dtype=jnp.int32)[None, :]
                 + jax.random.randint(ks[2], (BATCH, 1), 0, 1024, dtype=jnp.int32))
    dt = jnp.exp(jax.random.uniform(ks[15], (L, GDN_HEADS), f32, math.log(1e-3), math.log(1e-1)))
    return {
        'x': x,
        'c': c,
        'positions': positions,
        'w_ada': nrm(ks[3], (L, D, 6 * D), D, 0.5),
        'b_ada': 0.01 * jax.random.normal(ks[4], (L, 6 * D), f32),
        'norm_mix': gain(ks[5], (L, D)),
        'norm_ffn': gain(ks[6], (L, D)),
        'w_in': nrm(ks[7], (L, D, IN_WIDTH), D),
        'q_a_norm': gain(ks[8], (L, Q_LORA)),
        'kv_a_norm': gain(ks[9], (L, KV_LORA)),
        'w_uq': nrm(ks[10], (L, Q_LORA, MLA_HEADS * (QK_NOPE + QK_ROPE)), Q_LORA),
        'w_ukv': nrm(ks[11], (L, KV_LORA, MLA_HEADS * (QK_NOPE + V_HEAD)), KV_LORA),
        'w_o_mla': nrm(ks[12], (L, MLA_HEADS * V_HEAD, D), MLA_HEADS * V_HEAD),
        'conv_w': nrm(ks[13], (L, CONV_WIDTH, CONV_CH), CONV_WIDTH),
        'A_log': jnp.log(jax.random.uniform(ks[14], (L, GDN_HEADS), f32, 1.0, 16.0)),
        'dt_bias': dt + jnp.log(-jnp.expm1(-dt)),
        'gdn_norm': gain(ks[16], (L, GDN_DV)),
        'w_o_gdn': nrm(ks[17], (L, GDN_V, D), GDN_V),
        'w_o': nrm(ks[18], (L, D, D), D),
        'w_gate_up': nrm(ks[19], (L, D, 2 * D_FF), D),
        'w_down': nrm(ks[20], (L, D_FF, D), D_FF),
        'final_norm': gain(ks[21], (D,)),
    }

def first_block(x, c, positions, w_ada, b_ada, norm_mix, norm_ffn, w_in, q_a_norm, kv_a_norm,
              w_uq, w_ukv, w_o_mla, conv_w, A_log, dt_bias, gdn_norm, w_o_gdn, w_o,
              w_gate_up, w_down, final_norm):
    cos, sin = _rope_tables(positions)
    c_act = jax.nn.silu(c)
    for l in range(DEPTH):
        mod = c_act @ w_ada[l] + b_ada[l]
        sh_a, sc_a, gt_a, sh_f, sc_f, gt_f = [m[:, None, :] for m in jnp.split(mod, 6, axis=-1)]
        h = _rmsnorm(x, norm_mix[l]) * (1.0 + sc_a) + sh_a
        p = h @ w_in[l]
        c_q, c_kv, k_pe, q_g, k_g, v_g, z, b_logit, a_logit, gate_logits = _split_cols(p)
        y_a = _mla_branch(c_q, c_kv, k_pe, q_a_norm[l], kv_a_norm[l], w_uq[l], w_ukv[l], cos, sin) @ w_o_mla[l]
        qkv = jnp.concatenate([q_g, k_g, v_g], axis=-1)
        y_b = _gdn_branch(qkv, z, b_logit, a_logit, conv_w[l], A_log[l], dt_bias[l], gdn_norm[l]) @ w_o_gdn[l]
        g_a, g_b = jnp.split(jax.nn.sigmoid(gate_logits), 2, axis=-1)
        mix = (g_a * y_a + g_b * y_b) @ w_o[l]
        x = x + gt_a * mix
        h = _rmsnorm(x, norm_ffn[l]) * (1.0 + sc_f) + sh_f
        gate, up = jnp.split(h @ w_gate_up[l], 2, axis=-1)
        x = x + gt_f * ((jax.nn.silu(gate) * up) @ w_down[l])
    return _rmsnorm(x, final_norm)


N_MIXERS = 3
EXPAND = 2
D_INNER = EXPAND * D_MODEL
CHUNK_2 = 128
A_GROUPS = 8
A_GROUP_DIM = D_INNER // A_GROUPS
B_GROUPS = 8
B_GROUP_DIM = D_INNER // B_GROUPS
POOL_WINDOWS = (2, 4, 8, 16)
C_GROUPS = len(POOL_WINDOWS)
C_GROUP_DIM = D_INNER // C_GROUPS


def _layers_of_kind(kind):
    return len(range(kind, DEPTH, N_MIXERS))

def rmsnorm(x, g):
    xf = x.astype(jnp.float32)
    y = xf * lax.rsqrt(jnp.mean(xf * xf, axis=-1, keepdims=True) + EPS)
    return (y * g.astype(jnp.float32)).astype(x.dtype)

def gmlp_mixer(h, w_in, v_gain, w_s, b_s):
    bsz, seq, _ = h.shape
    z = h @ w_in
    u, v, gate = jnp.split(z, 3, axis=-1)
    u = jax.nn.gelu(u)
    v = rmsnorm(jax.nn.gelu(v), v_gain)
    vc = v.reshape(bsz, seq // CHUNK_2, CHUNK_2, A_GROUPS, A_GROUP_DIM)
    sv = jnp.einsum('gpq,bnqgc->bnpgc', w_s, vc) + b_s.T[None, None, :, :, None]
    y = u * sv.reshape(bsz, seq, D_INNER)
    return y, gate

def fourier_mixer(h, w_in, w_mix):
    bsz, seq, _ = h.shape
    z = h @ w_in
    xb, gate = jnp.split(z, 2, axis=-1)
    xg = xb.reshape(bsz, seq, B_GROUPS, B_GROUP_DIM).astype(jnp.float32)
    f = jnp.fft.fft2(xg, axes=(1, 3), norm="ortho").real.astype(xb.dtype)
    y = jnp.einsum('bsgc,gcd->bsgd', f, w_mix).reshape(bsz, seq, D_INNER)
    return y, gate

def pool_mixer(h, w_in, w_mix, scale):
    bsz, seq, _ = h.shape
    z = h @ w_in
    xc, gate = jnp.split(z, 2, axis=-1)
    xg = xc.reshape(bsz, seq, C_GROUPS, C_GROUP_DIM)
    t = jnp.arange(seq)
    pooled = []
    for gi, w in enumerate(POOL_WINDOWS):
        xi = xg[:, :, gi, :].astype(jnp.float32)
        csum = jnp.pad(lax.cumsum(xi, axis=1), ((0, 0), (1, 0), (0, 0)))
        lo = jnp.clip(t - w // 2, 0, seq - 1)
        hi = jnp.clip(t + w - 1 - w // 2, 0, seq - 1)
        wsum = jnp.take(csum, hi + 1, axis=1) - jnp.take(csum, lo, axis=1)
        cnt = (hi - lo + 1).astype(jnp.float32)[None, :, None]
        pooled.append(wsum / cnt - xi)
    p = jnp.stack(pooled, axis=2).astype(xc.dtype)
    y = jnp.einsum('bsgc,gcd->bsgd', p, w_mix).reshape(bsz, seq, D_INNER) * scale
    return y, gate

def second_inputs(seed: int = 0) -> dict:
    key = jax.random.key(seed)
    ks = jax.random.split(key, 20)
    na, nb, nc = _layers_of_kind(0), _layers_of_kind(1), _layers_of_kind(2)
    f32 = jnp.float32
    nrm = lambda k, shape, s: jax.random.normal(k, shape, f32) * s
    din = D_MODEL ** -0.5
    dout = D_INNER ** -0.5
    return {
        "x": jax.random.normal(ks[0], (BATCH, SEQ, D_MODEL), f32),
        "a_norm": 1.0 + nrm(ks[1], (na, D_MODEL), 0.05),
        "a_w_in": nrm(ks[2], (na, D_MODEL, 3 * D_INNER), din),
        "a_v_gain": 1.0 + nrm(ks[3], (na, D_INNER), 0.05),
        "a_w_s": nrm(ks[4], (na, A_GROUPS, CHUNK_2, CHUNK_2), 0.5 * CHUNK_2 ** -0.5),
        "a_b_s": 1.0 + nrm(ks[5], (na, A_GROUPS, CHUNK_2), 0.1),
        "a_w_out": nrm(ks[6], (na, D_INNER, D_MODEL), dout),
        "b_norm": 1.0 + nrm(ks[7], (nb, D_MODEL), 0.05),
        "b_w_in": nrm(ks[8], (nb, D_MODEL, 2 * D_INNER), din),
        "b_w_mix": nrm(ks[9], (nb, B_GROUPS, B_GROUP_DIM, B_GROUP_DIM), B_GROUP_DIM ** -0.5),
        "b_w_out": nrm(ks[10], (nb, D_INNER, D_MODEL), dout),
        "c_norm": 1.0 + nrm(ks[11], (nc, D_MODEL), 0.05),
        "c_w_in": nrm(ks[12], (nc, D_MODEL, 2 * D_INNER), din),
        "c_w_mix": nrm(ks[13], (nc, C_GROUPS, C_GROUP_DIM, C_GROUP_DIM), C_GROUP_DIM ** -0.5),
        "c_scale": 1.0 + nrm(ks[14], (nc, D_INNER), 0.1),
        "c_w_out": nrm(ks[15], (nc, D_INNER, D_MODEL), dout),
        "final_norm": 1.0 + nrm(ks[16], (D_MODEL,), 0.05),
    }

def second_block(x, a_norm, a_w_in, a_v_gain, a_w_s, a_b_s, a_w_out,
              b_norm, b_w_in, b_w_mix, b_w_out,
              c_norm, c_w_in, c_w_mix, c_scale, c_w_out, final_norm):
    for i in range(DEPTH):
        kind, j = i % N_MIXERS, i // N_MIXERS
        if kind == 0:
            h = rmsnorm(x, a_norm[j])
            y, gate = gmlp_mixer(h, a_w_in[j], a_v_gain[j], a_w_s[j], a_b_s[j])
            w_out = a_w_out[j]
        elif kind == 1:
            h = rmsnorm(x, b_norm[j])
            y, gate = fourier_mixer(h, b_w_in[j], b_w_mix[j])
            w_out = b_w_out[j]
        else:
            h = rmsnorm(x, c_norm[j])
            y, gate = pool_mixer(h, c_w_in[j], c_w_mix[j], c_scale[j])
            w_out = c_w_out[j]
        x = x + (y * jax.nn.silu(gate)) @ w_out
    return rmsnorm(x, final_norm)


def setup_inputs(seed=0):
    out = dict(first_inputs(seed))
    for name, value in second_inputs(seed + 1).items():
        if name != "x":
            out[name + "_2"] = value
    return out


def reference(
    x, c, positions, w_ada, b_ada, norm_mix, norm_ffn, w_in, q_a_norm, kv_a_norm, w_uq, w_ukv,
    w_o_mla, conv_w, A_log, dt_bias, gdn_norm, w_o_gdn, w_o, w_gate_up, w_down, final_norm,
    a_norm_2, a_w_in_2, a_v_gain_2, a_w_s_2, a_b_s_2, a_w_out_2, b_norm_2, b_w_in_2, b_w_mix_2,
    b_w_out_2, c_norm_2, c_w_in_2, c_w_mix_2, c_scale_2, c_w_out_2, final_norm_2,
):
    x = first_block(
        x, c, positions, w_ada, b_ada, norm_mix, norm_ffn, w_in, q_a_norm, kv_a_norm, w_uq,
        w_ukv, w_o_mla, conv_w, A_log, dt_bias, gdn_norm, w_o_gdn, w_o, w_gate_up, w_down,
        final_norm,
    )
    return second_block(
        x, a_norm_2, a_w_in_2, a_v_gain_2, a_w_s_2, a_b_s_2, a_w_out_2, b_norm_2, b_w_in_2,
        b_w_mix_2, b_w_out_2, c_norm_2, c_w_in_2, c_w_mix_2, c_scale_2, c_w_out_2, final_norm_2,
    )


_drawn_inputs = setup_inputs


def setup_inputs(seed=0):
    import zlib

    import numpy as np

    out = dict(_drawn_inputs(seed))
    spreads = {}
    factors = {'b_ada': 5.264,
     'norm_mix': 8.0,
     'norm_ffn': 8.0,
     'q_a_norm': 8.0,
     'kv_a_norm': 8.0,
     'gdn_norm': 8.0,
     'a_v_gain_2': 6.228}
    for name, (base, spread) in spreads.items():
        noise = np.random.default_rng([zlib.crc32(name.encode()), seed]).standard_normal(out[name].shape)
        drawn = base * np.exp(spread * noise) if base else spread * noise
        out[name] = jnp.asarray(drawn.astype(out[name].dtype))
    for name, factor in factors.items():
        out[name] = (out[name] * factor).astype(out[name].dtype)
    return out
```

```python
import numpy as np
import concourse.bass as bass
from concourse import mybir

F32 = mybir.dt.float32
FR = mybir.dt.float32r
I32 = mybir.dt.int32
ACT = mybir.ActivationFunctionType
ALU = mybir.AluOpType
AX = mybir.AxisListType.X

P = 128
T = 256
D = 2048
FF = 5632
DI = 4096
NH = 8
EPS = 1e-6
SCALE = 192.0 ** -0.5
KB = 256

C_ID, C_ONE, C_TRI, C_BLK, C_SEL, C_LVL, C_CM, C_INV, C_END = 0, 128, 256, 384, 512, 768, 1536, 1664, 1696

O_CQ, O_CKV, O_KPE, O_Q, O_K, O_V, O_Z, O_BA, O_GATE = 0, 512, 1024, 1088, 2112, 3136, 4160, 5184, 5200


def shape_constants():
    i = np.arange(P)
    same = (i[:, None] // 64) == (i[None, :] // 64)
    c = np.zeros((P, C_END), np.float32)
    c[:, C_ID:C_ID + P] = np.eye(P)
    c[:, C_ONE:C_ONE + P] = 1.0
    c[:, C_TRI:C_TRI + P] = same & (i[:, None] <= i[None, :])
    c[:, C_BLK:C_BLK + P] = same
    c[:64, C_SEL:C_SEL + P] = 1.0
    c[64:, C_SEL + P:C_SEL + 2 * P] = 1.0
    for n in range(6):
        s = 1 << n
        pair = (i[:, None] // (2 * s)) == (i[None, :] // (2 * s))
        m = pair & ((i[:, None] // s) % 2 == 0) & ((i[None, :] // s) % 2 == 1)
        c[:, C_LVL + n * P:C_LVL + (n + 1) * P] = m
    c[:, C_CM:C_CM + P] = np.where(i[None, :] <= i[:, None], 0.0, -1e30)
    inv = 1.0 / (10000.0 ** (np.arange(0, 64, 2, dtype=np.float64) / 64.0))
    c[:, C_INV:C_INV + 32] = inv.astype(np.float32)[None, :]
    return c


class Engines:

    def __init__(self, nc):
        self.nc = nc
        names = ["pe", "act", "dve", "pool", "sp"]
        self.engine = {"pe": nc.tensor, "act": nc.scalar, "dve": nc.vector, "pool": nc.gpsimd, "sp": nc.sync}
        self.count = {n: 0 for n in names}
        self.sem = {n: nc.alloc_semaphore("done_" + n) for n in names if n != "sp"}
        self.passed = {n: {} for n in names}
        self.dmas = {}

    def waits(self, eng, toks):
        flat = []

        def walk(t):
            if t is None:
                return
            if isinstance(t, tuple) and len(t) == 2 and isinstance(t[0], str):
                flat.append(t)
            else:
                for x in t:
                    walk(x)
        walk(toks)
        need = {}
        for s, v in flat:
            need[s] = max(need.get(s, 0), v)
        for s, v in need.items():
            if self.passed[eng].get(s, 0) < v:
                self.passed[eng][s] = v
                self.engine[eng].wait_ge(self.sem[s], v)

    def put(self, eng, fn, *toks):
        self.waits(eng, toks)
        self.count[eng] += 1
        fn(self.engine[eng]).then_inc(self.sem[eng], 1)
        return (eng, self.count[eng])

    def pe(self, fn, *toks):
        return self.put("pe", fn, *toks)

    def act(self, fn, *toks):
        return self.put("act", fn, *toks)

    def dve(self, fn, *toks):
        return self.put("dve", fn, *toks)

    def pool(self, fn, *toks):
        return self.put("pool", fn, *toks)

    def last(self, eng):
        return (eng, self.count[eng])

    def dma(self, name, out, src, *toks):
        key = "dma_" + name
        if key not in self.sem:
            self.sem[key] = self.nc.alloc_semaphore(key)
            self.dmas[key] = 0
        self.waits("sp", toks)
        self.dmas[key] += 16
        self.engine["sp"].dma_start(out, src).then_inc(self.sem[key], 16)
        return (key, self.dmas[key])


class Job:

    def __init__(self, name, loads, nkt, n, x, side, need, done, step=4, lazy=False):
        self.name, self.loads, self.nkt, self.n = name, loads, nkt, n
        self.x, self.side, self.need, self.done, self.step = x, side, need, done, step
        self.lazy = lazy


def program(nc, a, out):
    E = Engines(nc)
    pe, act, dve, pool, dma = E.pe, E.act, E.dve, E.pool, E.dma

    base = (nc.sbuf_base + 127) // 128 * 128
    at = [base]

    def place(name, words, dt=F32):
        t = nc.alloc_sbuf_tensor_at(name, [P, words], dt, offset=at[0])
        at[0] += words * 4
        return t[:, :]

    HTh = place("HTh", 16 * T, FR).rearrange("p (k t) -> p k t", t=T)
    HTl = place("HTl", 16 * T, FR).rearrange("p (k t) -> p k t", t=T)
    R2h = place("R2h", 8 * T, FR).rearrange("p (k t) -> p k t", t=T)
    R2l = place("R2l", 8 * T, FR).rearrange("p (k t) -> p k t", t=T)
    NHL = 4
    WH = place("WH", NHL * 1024, FR).rearrange("p (s w) -> p s w", s=NHL)
    WL = place("WL", NHL * 1024, FR).rearrange("p (s w) -> p s w", s=NHL)
    NR, NR1 = 3, 7
    RAW1 = (40, 48, 80, 88)
    RAW = place("RAW", NR * 2048).rearrange("p (s w) -> p s w", s=NR)
    CST = place("CST", C_END)
    COL = place("COL", 256)
    MOD = place("MOD", 96)
    GA = place("GA", 2048).rearrange("p (c b n) -> p c b n", c=2, b=2)
    ST = place("ST", 560)
    abase = at[0]
    A = place("A", 100 * KB)

    def over(name, kb, words, dt):
        return nc.alloc_sbuf_tensor_at(name, [P, words], dt, offset=abase + kb * 1024)[:, :]

    def ar(kb, words):
        return A[:, kb * KB:kb * KB + words]

    ident = CST[:, C_ID:C_ID + P]
    ones = CST[:, C_ONE:C_ONE + P]
    tri = CST[:, C_TRI:C_TRI + P]
    blk = CST[:, C_BLK:C_BLK + P]
    cm = CST[:, C_CM:C_CM + P]
    bank = [nc.alloc_psum_tensor(f"bank{i}", [P, 512], F32)[:, :] for i in range(8)]

    st_at = [0]

    def small(n):
        s = ST[:, st_at[0]:st_at[0] + n]
        st_at[0] += n
        assert st_at[0] <= 560
        return s

    units = []
    start_units = [0]

    def plan(jobs, extra, every):
        k = 0
        first = [("g", s + 512 * c, q) for c in range(4) for s in (2048, 0) for q in range(4)]
        units.extend(first[:8])
        for c in range(4):
            f = first[8 * c + 8:8 * c + 16]
            ws = [("w", j, 4 * c, 4) for j in jobs[:3]]
            units.extend(f[0:4] + ws[0:1] + f[4:6] + ws[1:2] + f[6:7] + ws[2:3] + f[7:8])
        start_units[0] = len(units)
        for j in jobs[3:]:
            for t0 in range(0, j.nkt, j.step):
                units.append(("w", j, t0, min(j.step, j.nkt - t0)))
                k += 1
                if extra and k % every == 0:
                    units.append(extra.pop(0))

    raw_free = [None] * NR1
    loaded = {}
    issued = [0]

    def raw_slot(i):
        return i % NR1 if i < start_units[0] else i % NR

    def raw_view(i, nkt, n):
        s = raw_slot(i)
        v = RAW[:, s, 0:nkt * n] if s < NR else ar(RAW1[s - NR], nkt * n)
        return v.rearrange("p (t n) -> p t n", n=n)

    def issue_loads(limit=10 ** 6):
        while issued[0] < min(limit, len(units), staged[0] + (NR1 if issued[0] < start_units[0] else NR)):
            i = issued[0]
            u = units[i]
            tok = None
            if u[0] == "w":
                _, j, t0, nkt = u
                for dst, src in j.loads(t0, nkt, raw_view(i, nkt, j.n)):
                    tok = dma(f"raw{raw_slot(i)}", dst, src, raw_free[raw_slot(i)])
            else:
                _, c0, q = u
                src = a["w_ada"].rearrange("(p t) n -> p t n", p=P)[:, 4 * q:4 * q + 4, c0:c0 + 512]
                tok = dma(f"raw{raw_slot(i)}", raw_view(i, 4, 512), src, raw_free[raw_slot(i)])
            loaded[i] = tok
            issued[0] += 1

    hl_free = [None] * NHL
    halves = []
    staged = [0, 0]
    cact = small(16)
    tk = {}
    ga_free = [None, None]
    bank_free = {i: None for i in range(4, 8)}
    ga_n = [0]
    pair_free = [None, None, None]
    current = [0]
    left, total = [0], [0]
    forced = [False]
    bg = []

    def mod_reduce(c0, tok, ga, wait, early):
        for n in range(wait):
            if n == wait - 2:
                tok = dve(lambda e: e.tensor_tensor(GA[:, ga, 0, :], GA[:, ga, 0, :], GA[:, ga, 1, :], ALU.add), tok)
            yield
        nh = 1 if wait > 1 else 2
        q = 1 - current[0]
        while not early and (pending[q] in bg or (not 2 <= left[0] <= min(5, total[0] - 2) and not forced[0])):
            yield
            q = 1 - current[0]
        b = bank[5] if early else bank[2 * q]
        free = bank_free[5] if early else pair_free[q]
        j0 = c0 // P

        def f(e):
            for m in range(4):
                for h in range(nh):
                    i = e.matmul(b[:, m:m + 1], GA[:, ga, h, m * P:(m + 1) * P], ones[:, 0:1], start=h == 0, stop=h == nh - 1)
            return i
        t = pe(f, tok, free, tk["cst"], tk["cols"])
        ga_free[ga] = t
        t = [act(lambda e, m=m: e.activation(MOD[:, j0 + m:j0 + m + 1], b[:, m:m + 1], ACT.Identity,
                                             bias=COL[:, j0 + m:j0 + m + 1]), t, free, tk["cols"]) for m in range(4)]
        if early:
            bank_free[5] = t
        else:
            pair_free[q] = [pair_free[q], t]
        tk[("mod", j0)] = t
        yield

    def stage_next():
        i, h = staged
        u = units[i]
        if u[0] == "g":
            _, c0, q = u
            rv = raw_view(i, 4, 512)
            tok = [None, None]
            ga = ga_n[0] % 2
            if q == 0 and ga_free[ga] == "busy":
                forced[0] = True
                while ga_free[ga] == "busy":
                    slot()
                forced[0] = False
            early = "ht_done" not in tk
            for t in range(4):
                col = cact[:, 4 * q + t:4 * q + t + 1]
                g = GA[:, ga, t % 2, :]
                if q == 0 and t < 2:
                    tok[t % 2] = act(lambda e, g=g, t=t, col=col: e.activation(g, rv[:, t, :], ACT.Copy, scale=col),
                                     loaded[i], tk["cact"], ga_free[ga])
                else:
                    if t == 2 and q == 0:
                        ga_first = list(tok)
                    before = tok[t % 2] or tk["ga"][t % 2]
                    tok[t % 2] = dve(lambda e, g=g, t=t, col=col: e.scalar_tensor_tensor(
                        out=g, in0=rv[:, t, :], scalar=col, in1=g, op0=ALU.mult, op1=ALU.add),
                        loaded[i], before)
            tk["ga"] = tok
            raw_free[raw_slot(i)] = list(tok) + ([ga_first] if q == 0 else [])
            if q == 3:
                ga_free[ga] = "busy"
                bg.append(mod_reduce(c0, tok, ga, 1 if early else 4, early))
                ga_n[0] += 1
            staged[0] += 1
            issue_loads()
            return
        _, j, t0, nkt = u
        hk = (nkt + 1) // 2
        k0, k1 = (0, hk) if h == 0 else (hk, nkt)
        s = len(halves) % NHL
        n = (k1 - k0) * j.n
        rv = raw_view(i, nkt, j.n)[:, k0:k1, :]
        hi = WH[:, s, 0:n].rearrange("p (t n) -> p t n", n=j.n)
        lo = WL[:, s, 0:n].rearrange("p (t n) -> p t n", n=j.n)
        t1 = act(lambda e: e.copy(hi, rv), loaded[i], hl_free[s])
        t2 = dve(lambda e: e.tensor_tensor(lo, rv, hi.bitcast(F32), ALU.subtract), t1, loaded[i], hl_free[s])
        halves.append((j, t0 + k0, k1 - k0, hi, lo, s, t2, t1))
        if h == 0 and nkt > 1:
            staged[1] = 1
        else:
            raw_free[raw_slot(i)] = [t1, t2]
            staged[0] += 1
            staged[1] = 0
            issue_loads()

    used = [0]

    def slot():
        for g in list(bg):
            try:
                next(g)
            except StopIteration:
                bg.remove(g)

    def finish(g):
        while g in bg:
            try:
                next(g)
            except StopIteration:
                bg.remove(g)

    def settle(key):
        n = 0
        while key not in tk:
            forced[0] = n > 8
            slot()
            n += 1
            assert n < 1000, key
        forced[0] = False

    pending = [None, None]

    def consume(j, b, free, one_bank=False):
        while len(halves) < used[0] + NHL and staged[0] < len(units):
            early = units[staged[0]][0] == "g" and "ht_done" not in tk
            stage_next()
            if early:
                slot()
        hj, t0, nk, hi, lo, s, t2, t1 = halves[used[0]]
        assert hj is j, (hj.name, j.name)
        xh, xl, x0 = j.x
        need = [j.need(t0 + k) for k in range(nk)]

        def f(e):
            for k in range(nk):
                kt = t0 + k
                first, last = kt == 0, kt == j.nkt - 1
                ah, al = xh[:, x0 + kt, :], xl[:, x0 + kt, :]
                if j.side == "tok":
                    for tt in range(2):
                        o = b[tt][:, 0:j.n]
                        s_ = slice(tt * P, tt * P + P)
                        e.matmul(o, ah[:, s_], hi[:, k, :], start=first and not (one_bank and tt), stop=False,
                                 skip_group_check=one_bank)
                        e.matmul(o, ah[:, s_], lo[:, k, :], start=False, stop=False, skip_group_check=one_bank)
                        i = e.matmul(o, al[:, s_], hi[:, k, :], start=False, stop=last, skip_group_check=one_bank)
                else:
                    for cb in range(j.n // P):
                        o = b[cb // 2][:, (cb % 2) * T:(cb % 2) * T + T]
                        s_ = slice(cb * P, cb * P + P)
                        e.matmul(o, hi[:, k, s_], ah, start=first and cb % 2 == 0, stop=False,
                                 skip_group_check=True)
                        e.matmul(o, hi[:, k, s_], al, start=False, stop=False, skip_group_check=True)
                        i = e.matmul(o, lo[:, k, s_], ah, start=False, stop=last, skip_group_check=True)
            return i
        tok = pe(f, t2, t1, need, free)
        hl_free[s] = tok
        used[0] += 1
        return nk, tok

    def retire(j, b, tok, pr):
        r = j.done(b, tok)
        if j.lazy:
            def whole():
                pair_free[pr] = yield from r
            pending[pr] = whole()
            bg.append(pending[pr])
        else:
            assert r is not None
            pair_free[pr] = r

    def run(j, own=None):
        if own:
            pr = 2
            b, free = (bank[6], bank[7]), [bank_free[6], bank_free[7]]
        else:
            current[0] = 1 - current[0]
            pr = current[0]
            finish(pending[pr])
            b, free = (bank[2 * pr], bank[2 * pr + 1]), pair_free[pr]
        done_k = 0
        left[0] = total[0] = (j.nkt + 1) // 2
        while done_k < j.nkt:
            nk, tok = consume(j, b, free)
            done_k += nk
            left[0] -= 1
            if done_k < j.nkt:
                slot()
        retire(j, b, tok, pr)
        if own:
            bank_free[6] = bank_free[7] = pair_free[2]
        slot()

    neg_half = small(16)
    tk["nh"] = pool(lambda e: e.memset(neg_half, -0.5))

    def rsqrt_of(ss, n, scale, outp, *toks):
        t = dve(lambda e: e.tensor_scalar(outp, ss, scale, EPS, ALU.mult, ALU.add), *toks)
        return pool(lambda e: e.tensor_tensor(outp, outp, neg_half[:, 0:n], ALU.pow), t, tk["nh"])

    craw = small(16)
    t_c = dma("c", craw, a["c"].rearrange("a (p t) -> p (a t)", p=P))
    X = ar(0, 2 * D).rearrange("p (b d) -> p b d", b=2)
    rows = [A[:, 60 * KB + P * i:60 * KB + P * (i + 1)] for i in range(3)]
    al = small(8)
    dtb = small(8)
    posi = nc.alloc_sbuf_tensor_at("posi", [P, 2], I32, offset=at[0])[:, :]
    at[0] += 32
    gn = place("GN", P)

    def small_loads():
        tk["cst"] = dma("cst", CST, a["cst"])
        dma("rows", rows[0][0:96, :], a["b_ada"].rearrange("(j p) -> j p", p=P))
        dma("rows", rows[1][0:96, :], a["conv_w"].rearrange("w (c p) -> (w c) p", p=P))
        r0 = 0
        for name in ("norm_mix", "norm_ffn", "a_norm_2", "q_a_norm", "kv_a_norm", "a_b_s_2"):
            v = a[name] if name == "a_b_s_2" else a[name].rearrange("(j p) -> j p", p=P)
            tk["rows"] = dma("rows", rows[2][r0:r0 + v.shape[0], :], v)
            r0 += v.shape[0]

    def last_loads():
        dma("vec", al, a["A_log"].rearrange("(a h) -> a h", a=1).to_broadcast([P, 8]))
        dma("vec", dtb, a["dt_bias"].rearrange("(a h) -> a h", a=1).to_broadcast([P, 8]))
        tk["vec"] = dma("vec", gn, a["gdn_norm"].rearrange("(a h) -> a h", a=1).to_broadcast([P, P]))
        with nc.allow_non_contiguous_dma(reason="256 positions"):
            tk["pos"] = dma("pos", posi, a["positions"].rearrange("a (b p) -> p (a b)", p=P))

    th = small(16)
    t = act(lambda e: e.activation(th, craw, ACT.Tanh, scale=0.5), t_c)
    t = dve(lambda e: e.scalar_tensor_tensor(out=cact, in0=th, scalar=1.0, in1=craw, op0=ALU.add, op1=ALU.mult), t, t_c)
    tk["cact"] = dve(lambda e: e.tensor_scalar(cact, cact, 0.5, None, ALU.mult), t)

    def start_loads():
        issue_loads(2)
        small_loads()
        issue_loads(4)
        for b in range(2):
            tk[("x", b)] = dma(f"x{b}", X[:, b, :], a["x"][b * P:(b + 1) * P, :])
        issue_loads()
        last_loads()

    def columns():
        for n, (r, m) in enumerate(((0, 96), (1, 96), (2, 64))):
            b = bank[4 + n]
            t = pe(lambda e, r=r, m=m, b=b: e.transpose(b[:, 0:m], rows[r][0:m, :], ident[0:m, 0:m]),
                   tk["rows"], tk["cst"])
            t = dve(lambda e, n=n, m=m, b=b: e.tensor_copy(COL[:, 96 * n:96 * n + m], b[:, 0:m]), t)
        t = dve(lambda e: e.tensor_scalar(COL[:, 96:192], COL[:, 96:192], 0.5, None, ALU.mult), t)
        tk["cols"] = t
        tk["gn"] = dve(lambda e: e.tensor_scalar(gn, gn, 0.5, None, ALU.mult), tk["vec"])

    colNM, colNF, colAN = COL[:, 192:208], COL[:, 208:224], COL[:, 224:240]
    colQA, colKA, colBS = COL[:, 240:244], COL[:, 244:248], COL[:, 248:256]

    def row_scale(Xv, junk, rs, *toks):
        ss = small(2)
        t = []
        for b in range(2):
            t.append(act(lambda e, b=b: e.activation(junk[:, b, :], Xv[:, b, :], ACT.Square,
                                                     accum_out=ss[:, b:b + 1]), [x[b] for x in toks]))
        return rsqrt_of(ss, 2, 1.0 / D, rs, t)

    def transposed(Xv, rs, xs, cA, cB, tmp, gate, prefix, free, banks, *toks):
        tb = []
        for b in range(2):
            tb.append(dve(lambda e, b=b: e.tensor_scalar(xs[:, b, :], Xv[:, b, :], rs[:, b:b + 1], None, ALU.mult), toks))
        tfree = [None, None]
        for g in range(8):
            bn = banks[g % len(banks)]
            bk = bank[bn]

            def f(e, g=g, bk=bk):
                for q in range(4):
                    kt, b = 2 * g + q // 2, q % 2
                    i = e.transpose(bk[:, q * P:(q + 1) * P], xs[:, b, kt * P:(kt + 1) * P], ident)
                return i
            t = pe(f, tb, bank_free[bn], tk["cst"])
            while gate and not all(x in tk for x in gate(2 * g)):
                yield
            w = [tk[x] for x in gate(2 * g)] if gate else None
            hi = HTh[:, 2 * g:2 * g + 2, :]
            lo = HTl[:, 2 * g:2 * g + 2, :]
            if cB is not None:
                tm = tmp[g % 2]
                ts = []
                for q in range(2):
                    kt = 2 * g + q
                    ts.append(dve(lambda e, q=q, kt=kt, bk=bk, tm=tm: e.tensor_scalar(
                        tm[:, q * T:(q + 1) * T], bk[:, q * T:(q + 1) * T], cA[:, kt:kt + 1], cB[:, kt:kt + 1],
                        ALU.mult, ALU.add), t, w, tfree[g % 2]))
                tm3 = tm.rearrange("p (k t) -> p k t", t=T)
                t1 = act(lambda e, hi=hi, tm3=tm3: e.copy(hi, tm3), ts, free)
                t2 = dve(lambda e, hi=hi, lo=lo, tm3=tm3: e.tensor_tensor(lo, tm3, hi.bitcast(F32), ALU.subtract), t1, free)
                bank_free[bn] = ts
                tfree[g % 2] = [t1, t2]
                r = [t1, t2]
            else:
                ks = [2 * g, 2 * g + 1]
                r = split_scaled([HTh[:, k, :] for k in ks], [HTl[:, k, :] for k in ks],
                                 [bk[:, q * T:(q + 1) * T] for q in range(2)], [cA[:, k:k + 1] for k in ks], t, w, free)
                bank_free[bn] = r
            tk[(prefix, 2 * g)] = r
            tk[(prefix, 2 * g + 1)] = r
            yield

    def split_scaled(dh, dl, src, scale, *toks):
        t1 = [act(lambda e, h=h, s=s, c=c: e.activation(h, s, ACT.Copy, scale=c), toks) for h, s, c in zip(dh, src, scale)]
        t2 = [dve(lambda e, h=h, l=l, s=s, c=c: e.scalar_tensor_tensor(
            out=l, in0=s, scalar=c, in1=h.bitcast(F32), op0=ALU.mult, op1=ALU.subtract), t1, toks)
            for h, l, s, c in zip(dh, dl, src, scale)]
        return [t1, t2]

    def split_out(dst_h, dst_l, src, scale, *toks):
        if scale is None:
            t1 = act(lambda e: e.copy(dst_h, src), toks)
            t2 = dve(lambda e: e.tensor_tensor(dst_l, src, dst_h.bitcast(F32), ALU.subtract), t1, toks)
        else:
            t1 = act(lambda e: e.activation(dst_h, src, ACT.Copy, scale=scale), toks)
            t2 = dve(lambda e: e.scalar_tensor_tensor(out=dst_l, in0=src, scalar=scale, in1=dst_h.bitcast(F32),
                                                      op0=ALU.mult, op1=ALU.subtract), t1, toks)
        return [t1, t2]

    cAm, cAf = small(16), small(16)
    cBm, cBf = MOD[:, 0:16], MOD[:, 48:64]
    colGA, colGF = MOD[:, 32:48], MOD[:, 80:96]

    def mod_scale(dst, col, m0, name):
        for q in range(4):
            while ("mod", m0 + 4 * q) not in tk:
                yield
            s = slice(4 * q, 4 * q + 4)
            m = MOD[:, m0 + 4 * q:m0 + 4 * q + 4]
            tk[(name, q)] = dve(lambda e, s=s, m=m: e.scalar_tensor_tensor(
                out=dst[:, s], in0=m, scalar=1.0, in1=col[:, s], op0=ALU.add, op1=ALU.mult),
                tk[("mod", m0 + 4 * q)], tk["cols"])

    R2hq, R2lq = R2h[:, 0:4, :], R2l[:, 0:4, :]
    qT = ar(24, 2048).rearrange("p (h t) -> p h t", t=T)
    kT = ar(32, 2048).rearrange("p (h t) -> p h t", t=T)
    VM = ar(40, 2048).rearrange("p (b n) -> p b n", b=2)
    QP = ar(48, 1024).rearrange("p (b n) -> p b n", b=2)
    QPT = ar(52, 1024).rearrange("p (h t) -> p h t", t=T)
    KPT = ar(56, 256)
    CQ = [ar(57, 1024).rearrange("p (b n) -> p b n", b=2), ar(61, 1024).rearrange("p (b n) -> p b n", b=2)]
    KP = ar(65, 256).rearrange("p (b n) -> p b n", b=2)
    COS = ar(66, 64).rearrange("p (b n) -> p b n", b=2)
    SIN = A[:, 66 * KB + 64:66 * KB + 128].rearrange("p (b n) -> p b n", b=2)
    RA = A[:, 66 * KB + 128:66 * KB + 256]
    RT = [ar(67, 256), ar(68, 256)]
    PR = [ar(69, 384), ar(71, 384)]
    PT = [ar(73, 384), ar(75, 384)]
    CV = [ar(77, 1024), ar(81, 1024)]
    CT = ar(85, 1024)
    SQ = ar(89, 1024)

    def rope_tables():
        posf = small(2)
        t = dve(lambda e: e.tensor_copy(posf, posi), tk["pos"])
        inv = CST[:, C_INV:C_INV + 32]
        ang, n, r2 = RA[:, 0:64].rearrange("p (b n) -> p b n", b=2), RA[:, 64:128].rearrange("p (b n) -> p b n", b=2), RT[0][:, 0:64].rearrange("p (b n) -> p b n", b=2)
        for b in range(2):
            t = dve(lambda e, b=b: e.tensor_scalar(ang[:, b, :], inv, posf[:, b:b + 1], None, ALU.mult), t, tk["cst"])
        magic = 1.5 * 2 ** 23
        p1, p2 = 6.28125, 0.0019350051879882812
        p3 = 2 * np.pi - p1 - p2
        for k in (4096.0, 1.0):
            t = dve(lambda e, k=k: e.tensor_scalar(n, ang, float(1.0 / (2 * np.pi * k)), magic, ALU.mult, ALU.add), t)
            t = dve(lambda e: e.tensor_scalar(n, n, magic, None, ALU.subtract), t)
            for c in (p1, p2, p3):
                t = dve(lambda e, c=c, k=k: e.scalar_tensor_tensor(out=ang, in0=n, scalar=float(-c * k), in1=ang,
                                                                   op0=ALU.mult, op1=ALU.add), t)
        lim = 3.1415925
        t = dve(lambda e: e.tensor_scalar(ang, ang, lim, -lim, ALU.min, ALU.max), t)
        t = dve(lambda e: e.tensor_scalar(r2, ang, -1.0, None, ALU.mult), t)
        t = dve(lambda e: e.tensor_tensor(r2, ang, r2, ALU.max), t)
        t = dve(lambda e: e.tensor_scalar(r2, r2, -1.0, float(np.pi / 2), ALU.mult, ALU.add), t)
        t1 = act(lambda e: e.activation(SIN, ang, ACT.Sin), t)
        tk["rope"] = act(lambda e: e.activation(COS, r2, ACT.Sin), t)

    def rope(dst, src, b, nh, *toks):
        c = COS[:, b, :].unsqueeze(1).to_broadcast([P, nh, 32])
        s = SIN[:, b, :].unsqueeze(1).to_broadcast([P, nh, 32])
        x1, x2 = src[:, :, 0:32], src[:, :, 32:64]
        m1 = RT[0][:, 0:nh * 32].rearrange("p (h n) -> p h n", n=32)
        m2 = RT[1][:, 0:nh * 32].rearrange("p (h n) -> p h n", n=32)
        w = [toks, tk["rope"], tk.get("rt"), tk["raw1"]]
        ta = dve(lambda e: e.tensor_tensor(m1, x1, c, ALU.mult), w)
        tb = dve(lambda e: e.tensor_tensor(m2, x2, s, ALU.mult), w)
        t = dve(lambda e: e.tensor_tensor(dst[:, :, 0:32], m1, m2, ALU.subtract), ta, tb)
        ta = dve(lambda e: e.tensor_tensor(m1, x2, c, ALU.mult), t)
        tb = dve(lambda e: e.tensor_tensor(m2, x1, s, ALU.mult), t)
        t2 = dve(lambda e: e.tensor_tensor(dst[:, :, 32:64], m1, m2, ALU.add), ta, tb)
        tk["rt"] = t2
        return [t, t2]

    def latent(which, col, b, tok):
        ss, rs = small(2), small(2)
        cq = CQ[which]
        ts = [act(lambda e, bb=bb: e.activation(cq[:, bb, :], b[bb][:, :], ACT.Square,
                                                accum_out=ss[:, bb:bb + 1]), tok) for bb in range(2)]
        yield
        t = rsqrt_of(ss, 2, 1.0 / 512, rs, ts)
        yield
        ts = [dve(lambda e, bb=bb: e.tensor_scalar(cq[:, bb, :], b[bb][:, :], rs[:, bb:bb + 1], None, ALU.mult), t, ts)
              for bb in range(2)]

        def rest():
            yield
            for g in range(2):
                bk = bank[5 + g]

                def f(e):
                    for q in range(4):
                        kt, bb = 2 * g + q // 2, q % 2
                        i = e.transpose(bk[:, q * P:(q + 1) * P], cq[:, bb, kt * P:(kt + 1) * P], ident)
                    return i
                t = pe(f, ts, bank_free[5 + g])
                ks = [4 * which + 2 * g + q for q in range(2)]
                r = split_scaled([R2h[:, k, :] for k in ks], [R2l[:, k, :] for k in ks],
                                 [bk[:, q * T:(q + 1) * T] for q in range(2)],
                                 [col[:, 2 * g + q:2 * g + q + 1] for q in range(2)], t)
                bank_free[5 + g] = r
                tk[("lat", which, 2 * g)] = r
                tk[("lat", which, 2 * g + 1)] = r
                yield
        bg.append(rest())
        return ts

    beta, g_, Gc, eG, eD = (small(16).rearrange("p (b h) -> p b h", b=2) for _ in range(5))
    sG = small(32).rearrange("p (b c h) -> p b c h", b=2, c=2)

    def small_out(b, tok):
        sm = [RT[0], RT[1]]
        ev = []
        eA = small(8)
        y, ab, tb = (small(16).rearrange("p (b h) -> p b h", b=2) for _ in range(3))
        r = []
        for bb in range(2):
            r += rope(KP[:, bb, 0:64].unsqueeze(1), b[bb][:, 0:64].unsqueeze(1), bb, 1, tok)
            yield
        t2 = [dve(lambda e, bb=bb: e.tensor_tensor(y[:, bb, :], b[bb][:, 72:80], dtb, ALU.add), tok, tk["vec"]) for bb in range(2)]
        tk_ = [act(lambda e, bb=bb: e.copy(KP[:, bb, 64:128], KP[:, bb, 0:64]), r) for bb in range(2)]
        t1 = [act(lambda e, bb=bb: e.activation(tb[:, bb, :], b[bb][:, 64:72], ACT.Tanh, scale=0.5), tok, t2) for bb in range(2)]
        yield
        tk["beta"] = dve(lambda e: e.tensor_scalar(beta, tb, 0.5, 0.5, ALU.mult, ALU.add), t1)
        t = dve(lambda e: e.tensor_scalar(ab, y, -1.0, None, ALU.mult), t2)
        t = dve(lambda e: e.tensor_tensor(ab, y, ab, ALU.max), t)
        t = act(lambda e: e.activation(ab, ab, ACT.Exp, scale=-1.0), t)
        t3 = act(lambda e: e.activation(eA, al, ACT.Exp), tk["vec"])
        yield
        t = dve(lambda e: e.tensor_scalar(ab, ab, 1.0, None, ALU.add), t)
        t = act(lambda e: e.activation(ab, ab, ACT.Ln), t)
        yield
        t = dve(lambda e: e.scalar_tensor_tensor(out=ab, in0=y, scalar=0.0, in1=ab, op0=ALU.max, op1=ALU.add), t)
        t = dve(lambda e: e.scalar_tensor_tensor(out=g_, in0=ab, scalar=-1.0,
                                                 in1=eA.unsqueeze(1).to_broadcast([P, 2, 8]),
                                                 op0=ALU.mult, op1=ALU.mult), t, t3)

        def rest(t):
            yield
            bk = bank[6]

            def f(e):
                for bb in range(2):
                    e.matmul(bk[:, 8 * bb:8 * bb + 8], tri, g_[:, bb, :], start=True, stop=True)
                    e.matmul(bk[:, 16 + 8 * bb:24 + 8 * bb], blk, g_[:, bb, :], start=True, stop=True)
                    for c in range(2):
                        o = 32 + 16 * bb + 8 * c
                        i = e.matmul(bk[:, o:o + 8], CST[:, C_SEL + c * P:C_SEL + (c + 1) * P], g_[:, bb, :],
                                     start=True, stop=True)
                return i
            t = pe(f, t, bank_free[6], tk["cst"])
            t4 = dve(lambda e: e.tensor_copy(Gc, bk[:, 0:16].rearrange("p (b h) -> p b h", b=2)), t)
            t5 = dve(lambda e: e.tensor_tensor(eD, bk[:, 16:32].rearrange("p (b h) -> p b h", b=2), Gc, ALU.subtract), t, t4)
            t6 = act(lambda e: e.activation(sG, bk[:, 32:64].rearrange("p (b c h) -> p b c h", b=2, c=2), ACT.Exp), t5)
            t7 = act(lambda e: e.activation(eG, Gc, ACT.Exp), t4)
            t8 = act(lambda e: e.activation(eD, eD, ACT.Exp), t5)
            bank_free[6] = [t4, t5, t6]
            tk["gate"] = [t4, t6, t7, t8, tk["beta"]]
            t = pe(lambda e: [e.transpose(bk[:, 64 + P * bb:64 + P * bb + P], KP[:, bb, :], ident) for bb in range(2)][-1],
                   tk_, r, t4, t5, t6)
            tk["kpt"] = dve(lambda e: e.tensor_copy(KPT, bk[:, 64:320]), t)
            bank_free[6] = tk["kpt"]
        bg.append(rest(t))
        return [r, tk_, t1, t2]

    def heads_T(dst, h0, key):
        def done(b, tok):
            r = []
            for i in range(2):
                d = dst[:, h0 + 2 * i:h0 + 2 * i + 2, :]
                s = b[i][:, :].rearrange("p (h t) -> p h t", t=T)
                if i == 0:
                    r.append(act(lambda e, d=d, s=s: e.copy(d, s), tok))
                else:
                    r.append(dve(lambda e, d=d, s=s: e.tensor_copy(d, s), tok))
            tk[key] = r
            return r
        return done

    def q_pe_out(b, tok):
        r = []
        for bb in range(2):
            r += rope(QP[:, bb, :].rearrange("p (h n) -> p h n", n=64), b[bb][:, :].rearrange("p (h n) -> p h n", n=64), bb, 8, tok)
            yield

        def rest():
            yield
            bk = bank[4]
            for g in range(2):
                bk = bank[4 + g]

                def f(e, g=g, bk=bk):
                    for q in range(4):
                        hp, bb = 2 * g + q // 2, q % 2
                        i = e.transpose(bk[:, q * P:(q + 1) * P], QP[:, bb, hp * P:(hp + 1) * P], ident)
                    return i
                t = pe(f, r, bank_free[4 + g])
                t = act(lambda e, g=g, bk=bk: e.copy(QPT[:, 2 * g:2 * g + 2, :], bk.rearrange("p (h t) -> p h t", t=T)), t, tk["raw1"])
                bank_free[4 + g] = t
            tk["qpt"] = t
        bg.append(rest())
        return r

    def v_out(c):
        def done(b, tok):
            r = [act(lambda e: e.copy(VM[:, 0, 512 * c:512 * c + 512], b[0][:, :]), tok, tk["raw1"]),
                 dve(lambda e: e.tensor_copy(VM[:, 1, 512 * c:512 * c + 512], b[1][:, :]), tok, tk["raw1"])]
            tk[("vm", c)] = r
            return r
        return done

    mx, nmx, lsum, rl = (small(16) for _ in range(4))

    def attention():
        for k in ("qpt", "kpt", ("qT", 0), ("qT", 1), ("kT", 0), ("kT", 1), ("vm", 0), ("vm", 1)):
            while k not in tk:
                yield
        yield
        yield
        lat_free = E.last("pe")
        ready = [tk[k] for k in ("qpt", "kpt", ("qT", 0), ("qT", 1), ("kT", 0), ("kT", 1), ("vm", 0), ("vm", 1))]
        sm, pt = {}, {}
        prf, ptf = [None, None], [None, None]
        for i in range(NH + 2):
            if i >= 2:
                h = i - 2
                bk = bank[7]

                def f(e, h=h):
                    p = PT[h % 2]
                    e.matmul(bk[:, 0:P], VM[:, 0, h * P:(h + 1) * P], p[:, 0:P], start=True, stop=True)
                    e.matmul(bk[:, P:T], VM[:, 0, h * P:(h + 1) * P], p[:, P:2 * P], start=True, stop=False)
                    return e.matmul(bk[:, P:T], VM[:, 1, h * P:(h + 1) * P], p[:, 2 * P:3 * P], start=False, stop=True)
                t = pe(f, pt[h], bank_free[7])
                ptf[h % 2] = t
                r = split_out(R2h[:, h, :], R2l[:, h, :], bk[:, 0:T], None, t, lat_free)
                bank_free[7] = r
                tk[("omla", h)] = r
            if 1 <= i < NH + 1:
                h = i - 1
                bk = bank[6]

                def f(e, h=h):
                    for q in range(3):
                        i_ = e.transpose(bk[:, q * P:(q + 1) * P], PR[h % 2][:, q * P:(q + 1) * P], ident)
                    return i_
                t = pe(f, sm[h], bank_free[6])
                prf[h % 2] = t
                pt[h] = dve(lambda e, h=h: e.tensor_copy(PT[h % 2], bk[:, 0:384]), t, ptf[h % 2])
                bank_free[6] = pt[h]
            if i < NH:
                h = i
                bn = 4 + h % 2
                bk = bank[bn]
                pb = 64 * (h % 2)

                def f(e, h=h, bk=bk, pb=pb):
                    for blk_, c0, n in ((0, 0, P), (1, P, T)):
                        q = slice(blk_ * P, blk_ * P + P)
                        o = bk[:, c0:c0 + n]
                        e.matmul(o, qT[:, h, q], kT[:, h, 0:n], start=True, stop=False, skip_group_check=True)
                        e.matmul(o, QPT[pb:pb + 64, h // 2, q], KPT[pb:pb + 64, 0:n], start=False, stop=False,
                                 skip_group_check=True)
                        i_ = e.matmul(bk[:, c0 + n - P:c0 + n], ident, cm, start=False, stop=True,
                                      skip_group_check=True)
                    return i_
                t = pe(f, ready, bank_free[bn])
                ts, te = [], []
                for k, c0, n in ((0, 0, P), (1, P, T)):
                    ts.append(dve(lambda e, h=h, k=k, c0=c0, n=n, bk=bk: e.tensor_reduce(
                        mx[:, 2 * h + k:2 * h + k + 1], bk[:, c0:c0 + n], AX, ALU.max), t))
                tn = dve(lambda e, h=h: e.tensor_scalar(nmx[:, 2 * h:2 * h + 2], mx[:, 2 * h:2 * h + 2], -SCALE, None,
                                                        ALU.mult), ts)
                for k, c0, n in ((0, 0, P), (1, P, T)):
                    te.append(act(lambda e, h=h, k=k, c0=c0, n=n, bk=bk: e.activation(
                        PR[h % 2][:, c0:c0 + n], bk[:, c0:c0 + n], ACT.Exp, bias=nmx[:, 2 * h + k:2 * h + k + 1],
                        scale=SCALE, accum_out=lsum[:, 2 * h + k:2 * h + k + 1]), tn, prf[h % 2]))
                tr = dve(lambda e, h=h: e.reciprocal(rl[:, 2 * h:2 * h + 2], lsum[:, 2 * h:2 * h + 2]), te)
                sm[h] = [dve(lambda e, h=h, k=k, c0=c0, n=n: e.tensor_scalar(
                    PR[h % 2][:, c0:c0 + n], PR[h % 2][:, c0:c0 + n], rl[:, 2 * h + k:2 * h + k + 1], None,
                    ALU.mult), tr) for k, c0, n in ((0, 0, P), (1, P, T))]
                bank_free[bn] = [te]
            yield
        tk["attention"] = [E.last("pe"), E.last("act"), E.last("dve")]

    NAT = {k: ar(8 * i, 2048).rearrange("p (b h d) -> p b h d", b=2, h=8) for i, k in enumerate("qkv")}
    cv_free = [None, None]
    ct_free = [None]
    cvn = [0]

    def conv_out(kind, c):
        ct0 = {"q": 0, "k": 8, "v": 16}[kind] + 4 * c

        def done(b, tok):
            n = cvn[0] % 2
            cvn[0] += 1
            cv = CV[n]
            ends = []
            for i in range(4):
                u = b[i // 2][:, (i % 2) * T:(i % 2) * T + T]
                o = cv[:, i * T:(i + 1) * T]

                def w(k, i=i):
                    j = 96 + 24 * k + ct0 + i
                    return COL[:, j:j + 1]
                ends.append((u, o, w))
            ts, last = [], [None, None]
            for i in range(2):
                for q in range(2):
                    u, o, w = ends[2 * q + i]
                    last[q] = act(lambda e: e.activation(o, u, ACT.Copy, scale=w(3)), tok, cv_free[n], tk["cols"], last[q])
                for s in (1, 2, 3):
                    for q in range(2):
                        u, o, w = ends[2 * q + i]
                        last[q] = dve(lambda e: e.scalar_tensor_tensor(
                            out=o[:, s:T], in0=u[:, 0:T - s], scalar=w(3 - s), in1=o[:, s:T], op0=ALU.mult, op1=ALU.add), last[q])
                ts += last
                yield

            def rest():
                yield
                t = act(lambda e: e.activation(CT, cv, ACT.Tanh), ts, ct_free[0])
                yield
                t = dve(lambda e: e.scalar_tensor_tensor(out=cv, in0=CT, scalar=1.0, in1=cv, op0=ALU.add, op1=ALU.mult), t)
                ct_free[0] = t
                for _ in range(3):
                    yield
                rr = []
                for bb in range(2):
                    bn = 4 + bb
                    bk = bank[bn]

                    def f(e, bb=bb, bk=bk):
                        for i in range(4):
                            i_ = e.transpose(bk[:, i * P:(i + 1) * P], cv[:, i * T + bb * P:i * T + bb * P + P], ident)
                        return i_
                    tt = pe(f, t, bank_free[bn])
                    cv_free[n] = tt
                    d = NAT[kind][:, bb, 4 * c:4 * c + 4, :]
                    s = bk.rearrange("p (h d) -> p h d", d=P)
                    rr.append(act(lambda e, d=d, s=s: e.copy(d, s), tt, tk["ht_done"]))
                    bank_free[bn] = rr[-1]
                if kind == "v":
                    tk[("nat", kind, c)] = rr
                    return
                yield
                t0 = []
                for bb in range(2):
                    d = NAT[kind][:, bb, 4 * c:4 * c + 4, :]
                    ss, rs = small(4), small(4)
                    sq = SQ[:, 512 * bb:512 * bb + 512].rearrange("p (h d) -> p h d", d=P)
                    t1 = act(lambda e, d=d, sq=sq: e.activation(sq, d, ACT.Square), rr[bb], tk.get(("sq", bb)))
                    t1 = dve(lambda e, sq=sq, ss=ss: e.tensor_reduce(ss, sq, AX, ALU.add), t1)
                    tk[("sq", bb)] = t1
                    t0.append((d, rs, rsqrt_of(ss, 4, 1.0, rs, t1)))
                yield
                for bb, (d, rs, t1) in enumerate(t0):
                    if kind == "q":
                        t1 = dve(lambda e, rs=rs: e.tensor_scalar(rs, rs, float(P ** -0.5), None, ALU.mult), t1)
                    rr[bb] = dve(lambda e, d=d, rs=rs: e.tensor_tensor(
                        d, d, rs.unsqueeze(2).to_broadcast([P, 4, P]), ALU.mult), t1, rr[bb])
                tk[("nat", kind, c)] = rr
            bg.append(rest())
            return ts
        return done

    SS = [ar(96, 512).rearrange("p (h d) -> p h d", d=P), ar(98, 512).rearrange("p (h d) -> p h d", d=P)]
    s_tok = [None, None]

    def bc4(col):
        return col.unsqueeze(2).to_broadcast([P, 4, P])

    def bm4(mat):
        return mat.unsqueeze(1).to_broadcast([P, 4, P])

    def cell(tt, g):
        s = [ar(64 + 16 * g + 2 * i, 512).rearrange("p (h d) -> p h d", d=P) for i in range(8)]
        na, nb = 4 + 2 * g, 5 + 2 * g
        a_, b_ = (bank[n].rearrange("p (h d) -> p h d", d=P) for n in (na, nb))
        hs = slice(4 * g, 4 * g + 4)
        q, k, v = (NAT[x][:, tt, hs, :] for x in "qkv")
        S = SS[g]
        gate = tk["gate"]
        nat = [tk[("nat", x, h)] for x in "qkv" for h in range(2)]
        start = [tk.get(("cell", tt - 1, g)), tk["attention"], nat, gate]

        def each(f):
            def run_(e):
                for h in range(4):
                    i = f(e, h)
                return i
            return run_
        fa, fb = bank_free[na], bank_free[nb]
        t_gt = dve(lambda e: e.tensor_tensor(s[4], bm4(tri), bc4(g_[:, tt, hs]), ALU.mult), start)
        t_kb = dve(lambda e: e.tensor_tensor(s[7], k, bc4(beta[:, tt, hs]), ALU.mult), start)
        yield
        t1 = pe(lambda e: e.matmul(bank[na], ones, s[4].rearrange("p h d -> p (h d)"), start=True, stop=True), t_gt, fa)
        t2 = pe(each(lambda e, h: e.transpose(b_[:, h, :], k[:, h, :], ident)), fb)
        t3 = dve(lambda e: e.tensor_tensor(s[5], a_, bc4(Gc[:, tt, hs]), ALU.subtract), t1, start)
        t3b = dve(lambda e: e.tensor_scalar(s[5], s[5], 0.0, None, ALU.min), t3)
        t4 = act(lambda e: e.copy(s[0], b_), t2, start)
        t5 = act(lambda e: e.activation(s[5], s[5], ACT.Exp), t3b)
        yield
        t6 = pe(each(lambda e, h: e.transpose(a_[:, h, :], s[7][:, h, :], ident)), t_kb, t3)
        t7 = pe(each(lambda e, h: e.transpose(b_[:, h, :], q[:, h, :], ident)), t4)
        t_dec = dve(lambda e: e.tensor_tensor(s[4], s[5], bm4(tri), ALU.mult), t5, t1)
        t8 = dve(lambda e: e.tensor_copy(s[1], a_), t6, start)
        t9 = act(lambda e: e.copy(s[2], b_), t7, start)
        yield
        t10 = pe(each(lambda e, h: e.matmul(a_[:, h, :], s[0][:, h, :], s[1][:, h, :], start=True, stop=True)), t4, t8)
        t11 = pe(each(lambda e, h: e.matmul(b_[:, h, :], s[0][:, h, :], s[2][:, h, :], start=True, stop=True)), t9)
        t_qg = dve(lambda e: e.tensor_tensor(q, q, bc4(eG[:, tt, hs]), ALU.mult), t7)
        t_LT = dve(lambda e: e.tensor_tensor(s[5], a_, s[4], ALU.mult), t10, t_dec)
        t_at = dve(lambda e: e.tensor_tensor(s[4], b_, s[4], ALU.mult), t11, t_LT)
        t_m = dve(lambda e: e.tensor_tensor(s[6], s[5], bm4(CST[:, C_LVL:C_LVL + P]), ALU.mult), t_LT, start)
        t_XT = dve(lambda e: e.tensor_tensor(s[1], bm4(ident), s[6], ALU.subtract), t_m, t10)
        yield
        t12 = pe(each(lambda e, h: e.transpose(a_[:, h, :], q[:, h, :], ident)), t_qg, t_LT)
        t13 = pe(each(lambda e, h: e.matmul(b_[:, h, :], s[6][:, h, :], ident, start=True, stop=True)), t_m, t_at)
        t_qgT = act(lambda e: e.copy(s[3], a_), t12, start)
        t_X = dve(lambda e: e.tensor_tensor(s[0], bm4(ident), b_, ALU.subtract), t13, t11)
        t_m = dve(lambda e: e.tensor_tensor(s[6], s[5], bm4(CST[:, C_LVL + P:C_LVL + 2 * P]), ALU.mult), t13, t_XT)
        t_kg = dve(lambda e: e.tensor_tensor(s[7], s[7], bc4(eG[:, tt, hs]), ALU.mult), t6)
        fa, fb = t_qgT, t_X
        for lv in range(1, 6):
            yield
            ty = pe(each(lambda e, h: e.matmul(a_[:, h, :], s[6][:, h, :], s[0][:, h, :], start=True, stop=True)), t_m, t_X, fa)
            t_Y = act(lambda e: e.copy(s[2], a_), ty, t11)
            if lv < 5:
                t_m = dve(lambda e, lv=lv: e.tensor_tensor(
                    s[6], s[5], bm4(CST[:, C_LVL + (lv + 1) * P:C_LVL + (lv + 2) * P]), ALU.mult), ty)
            if lv == 1:
                t_kd = dve(lambda e: e.tensor_tensor(k, k, bc4(eD[:, tt, hs]), ALU.mult), t2)
            if lv == 2:
                t_vb = dve(lambda e: e.tensor_tensor(v, v, bc4(beta[:, tt, hs]), ALU.mult), start)
            yield
            tb = pe(each(lambda e, h: e.matmul(b_[:, h, :], s[2][:, h, :], s[1][:, h, :], start=True, stop=True)), t_Y, t_XT, fb)
            if lv < 5:
                ta = pe(each(lambda e, h: e.matmul(a_[:, h, :], s[1][:, h, :], s[2][:, h, :], start=True, stop=True)), t_Y)
            t_XT = dve(lambda e: e.tensor_tensor(s[1], s[1], b_, ALU.subtract), tb, ta if lv < 5 else None)
            fb = t_XT
            if lv < 5:
                t_X = dve(lambda e: e.tensor_tensor(s[0], s[0], a_, ALU.subtract), ta)
                fa = t_X
            else:
                fa = t_Y
        yield
        tu = pe(each(lambda e, h: e.matmul(a_[:, h, :], s[1][:, h, :], v[:, h, :], start=True, stop=True)), t_XT, t_vb, fa)
        tw = pe(each(lambda e, h: e.matmul(b_[:, h, :], s[7][:, h, :], s[1][:, h, :], start=True, stop=True)), t_kg, fb)
        t_u = act(lambda e: e.copy(s[5], a_), tu)
        t_w = dve(lambda e: e.tensor_copy(s[6], b_), tw)
        fa, fb = t_u, t_w
        tS = s_tok[g]
        for c in range(2):
            r = slice(64 * c, 64 * c + 64)
            first = tt == 0 and c == 0
            if not first:
                yield
                t = pe(each(lambda e, h, r=r: e.matmul(a_[r, h, :], s[6][:, h, r], S[:, h, :], start=True, stop=True)), t_w, tS, fa)
                t_v = dve(lambda e, r=r: e.tensor_tensor(s[2][r], s[5][r], a_[r], ALU.subtract), t, t_u, tb)
            else:
                t_v = dve(lambda e, r=r: e.tensor_copy(s[2][r], s[5][r]), t_u, tb)
            yield

            def fo(e, h, r=r, first=first):
                if not first:
                    e.matmul(b_[r, h, :], s[3][:, h, r], S[:, h, :], start=True, stop=False)
                return e.matmul(b_[r, h, :], s[4][r, h, r], s[2][r, h, :], start=first, stop=True)
            to = pe(each(fo), t_v, t_qgT, t_at, fb)
            td = pe(each(lambda e, h, r=r: e.matmul(a_[:, h, :], k[r, h, :], s[2][r, h, :], start=True, stop=True)), t_kd, t_v, fa)
            if first:
                tS = dve(lambda e: e.tensor_copy(S, a_), td, tk["attention"])
            else:
                tS = dve(lambda e, c=c: e.tensor_tensor(S, S, bc4(sG[:, tt, c, hs]), ALU.mult), to, td, tS)
                tS = dve(lambda e: e.tensor_tensor(S, S, a_, ALU.add), td, tS)
            fa = tS
            s_tok[g] = tS
        yield
        t_o = act(lambda e: e.copy(q, b_), to, t12)
        bank_free[na], bank_free[nb] = fa, t_o
        ss, rs = small(4), small(4)
        t = act(lambda e: e.activation(s[0], q, ACT.Square), t_o, ty)
        t = dve(lambda e: e.tensor_reduce(ss, s[0], AX, ALU.add), t)
        t_r = rsqrt_of(ss, 4, 1.0 / P, rs, t)
        yield
        t = dve(lambda e: e.tensor_tensor(q, q, bc4(rs), ALU.mult), t_r, t_o, t)
        t = dve(lambda e: e.tensor_tensor(q, q, bm4(gn), ALU.mult), t, tk["gn"])
        tk[("o", tt, g)] = t
        tk[("cell", tt, g)] = [E.last("pe"), E.last("act"), E.last("dve")]
        if tt == 0:
            bg.append(cell(1, g))

    Z = ar(56, 2048).rearrange("p (b n) -> p b n", b=2)
    M = ar(24, 4096).rearrange("p (b n) -> p b n", b=2)
    GB = ar(40, 4096).rearrange("p (b n) -> p b n", b=2)

    def z_out(c):
        def done(b, tok):
            r, e_ = [], []
            for bb in range(2):
                z = Z[:, bb, 512 * c:512 * c + 512]
                t = act(lambda e, z=z, bb=bb: e.activation(z, b[bb][:, :], ACT.Tanh, scale=0.5), tok, tk["attention"])
                r.append(dve(lambda e, z=z, bb=bb: e.scalar_tensor_tensor(
                    out=z, in0=z, scalar=1.0, in1=b[bb][:, :], op0=ALU.add, op1=ALU.mult), t, tok))
            tk[("z", c)] = r
            return r
        return done

    def gdn_final():
        for tt in range(2):
            for g in range(2):
                while ("cell", 1, 0) not in tk or ("cell", 1, 1) not in tk or ("z", g) not in tk or "omla_used" not in tk:
                    yield
                o = NAT["q"][:, tt, 4 * g:4 * g + 4, :]
                z = Z[:, tt, 512 * g:512 * g + 512].rearrange("p (h d) -> p h d", d=P)
                t = dve(lambda e, o=o, z=z: e.tensor_tensor(o, o, z, ALU.mult), tk[("o", tt, g)], tk[("z", g)])
                yield
                bn = 4 + (2 * tt + g)
                bk = bank[bn].rearrange("p (h d) -> p h d", d=P)

                def f(e, o=o, bk=bk):
                    for h in range(4):
                        i = e.transpose(bk[:, h, :], o[:, h, :], ident)
                    return i
                t = pe(f, t, bank_free[bn])
                r = split_out(R2h[:, 4 * g:4 * g + 4, tt * P:tt * P + P], R2l[:, 4 * g:4 * g + 4, tt * P:tt * P + P],
                              bk, None, t, tk["omla_used"])
                bank_free[bn] = r
                tk[("ogdn", tt, g)] = r
                tk["o_read"] = t

    def ga_out(c):
        def done(b, tok):
            settle("attention")
            r = [act(lambda e, bb=bb: e.activation(M[:, bb, 512 * c:512 * c + 512], b[bb][:, :], ACT.Tanh, scale=0.5),
                     tok, tk["attention"]) for bb in range(2)]
            tk[("ga", c)] = r
            return r
        return done

    def half_sum(dst, x, t_in, *toks):
        return dve(lambda e: e.scalar_tensor_tensor(out=dst, in0=t_in, scalar=1.0, in1=x, op0=ALU.add, op1=ALU.mult), toks)

    def omla_out(c):
        def done(b, tok):
            r = [half_sum(M[:, bb, 512 * c:512 * c + 512], b[bb][:, :], M[:, bb, 512 * c:512 * c + 512],
                          tok, tk[("ga", c)]) for bb in range(2)]
            tk[("m", c)] = r
            if c == 3:
                tk["omla_used"] = tok
            return r
        return done

    def gb_out(c):
        def done(b, tok):
            r = [act(lambda e, bb=bb: e.activation(GB[:, bb, 512 * c:512 * c + 512], b[bb][:, :], ACT.Tanh, scale=0.5),
                     tok, tk["attention"]) for bb in range(2)]
            tk[("gb", c)] = r
            if c == 3:
                tk["ht_free"] = tok
            return r
        return done

    def to_hl(src, dh, dl, k0, key, free, *toks, scale=None):
        yield
        yield
        for g in range(2):
            bn = 4 + to_hl_n[0] % 4
            to_hl_n[0] += 1
            bk = bank[bn]

            def f(e, g=g, bk=bk):
                for q in range(4):
                    kt, bb = 2 * g + q // 2, q % 2
                    i = e.transpose(bk[:, q * P:(q + 1) * P], src[:, bb, kt * P:(kt + 1) * P], ident)
                return i
            t = pe(f, toks, bank_free[bn])
            r = split_out(dh[:, k0 + 2 * g:k0 + 2 * g + 2, :], dl[:, k0 + 2 * g:k0 + 2 * g + 2, :],
                          bk.rearrange("p (k t) -> p k t", t=T), scale, t, free)
            bank_free[bn] = r
            for q in range(2):
                tk[(key, k0 + 2 * g + q)] = r
            yield
        src_read[id(src)] = t
    to_hl_n = [0]
    src_read = {}

    MX = [ar(64, 1024).rearrange("p (b n) -> p b n", b=2), ar(68, 1024).rearrange("p (b n) -> p b n", b=2)]

    def ogdn_out(c):
        def done(b, tok):
            mx_ = MX[c % 2]
            r, r2 = [], []
            for bb in range(2):
                t = half_sum(mx_[:, bb, :], b[bb][:, :], GB[:, bb, 512 * c:512 * c + 512], tok, tk[("gb", c)],
                             src_read.get(id(mx_)), tk[("cell", 1, 0)], tk[("cell", 1, 1)])
                r.append(t)
                m = M[:, bb, 512 * c:512 * c + 512]
                r2.append(dve(lambda e, m=m, bb=bb: e.tensor_tensor(mx_[:, bb, :], mx_[:, bb, :], m, ALU.add), t, tk[("m", c)]))
            bg.append(to_hl(mx_, HTh, HTl, 4 * c, "mix", tk["ht_free"], r2, scale=0.5))
            return r
        return done

    GT = ar(56, 2048)
    DG = ar(96, 512).rearrange("p (h d) -> p h d", d=P)

    def spread(col, m0, name, *toks):
        for c in range(4):
            while ("mod", m0 + 4 * c) not in tk:
                yield
            t = dve(lambda e, c=c: e.tensor_tensor(DG, bm4(ident), bc4(col[:, 4 * c:4 * c + 4]), ALU.mult),
                    tk[("mod", m0 + 4 * c)], toks, tk.get("dg"))
            yield
            bk = bank[7]
            t = pe(lambda e: e.matmul(bk, ones, DG.rearrange("p h d -> p (h d)"), start=True, stop=True), t, bank_free[7])
            tk["dg"] = t
            t = act(lambda e, c=c: e.copy(GT[:, 512 * c:512 * c + 512], bk), t, toks)
            bank_free[7] = t
            tk[(name, c)] = t
            yield

    TO = [ar(76, 512), ar(78, 512)]

    def residual(c, gt, xtok, key, turn=None):
        def done(b, tok):
            if gt:
                settle((gt, c))
            r, rx = [], []
            for bb in range(2):
                xv = X[:, bb, 512 * c:512 * c + 512]
                if gt:
                    t = dve(lambda e, bb=bb: e.tensor_tensor(TO[bb], b[bb][:, :], GT[:, 512 * c:512 * c + 512], ALU.mult),
                            tok, tk[(gt, c)], tk.get(("to", bb)), tk.get("to_free"))
                    r.append(t)
                    t = dve(lambda e, bb=bb, xv=xv: e.tensor_tensor(xv, xv, TO[bb], ALU.add), t, tk[xtok(bb)], tk.get(("xr", c, bb)))
                    tk[("to", bb)] = t
                else:
                    t = dve(lambda e, bb=bb, xv=xv: e.tensor_tensor(xv, xv, b[bb][:, :], ALU.add), tok, tk[xtok(bb)], tk.get(("xr", c, bb)))
                    r.append(t)
                tk[("xr", c, bb)] = t
                rx.append(t)
            tk[(key, c)] = rx
            if turn:
                turn["bg"].append(turn_chunk(turn, c, rx))
                bg.append(turn["bg"][-1])
            return r
        return done

    XT = ar(80, 4096).rearrange("p (k t) -> p k t", t=T)
    DR = ar(99, 256)
    JK = [ar(64, 512), ar(66, 512)]
    TM = [ar(68, 512), ar(70, 512)]

    def new_turn(cA, gate, factor):
        return dict(s1=small(8).rearrange("p (b c) -> p b c", b=2), s2=small(8).rearrange("p (b c) -> p b c", b=2),
                    cA=cA, gate=gate, factor=factor, bg=[], sq=[], xt={}, x={}, both=factor is not None and cA is not None)

    def turn_chunk(S, c, rx):
        cs = slice(512 * c, 512 * c + 512)
        w = S["free"]

        def squares(acc, toks):
            t = []
            for bb in range(2):
                t.append(act(lambda e, bb=bb: e.activation(JK[bb], X[:, bb, cs], ACT.Square, accum_out=acc[:, bb, c:c + 1]),
                             toks[bb], w, S.get(("jk", bb))))
                S[("jk", bb)] = t[-1]
            S["sq"].append(t)
            return t
        t = squares(S["s1"], rx)
        xt = rx
        if S["factor"] is not None:
            xt = [dve(lambda e, bb=bb: e.tensor_tensor(X[:, bb, cs], X[:, bb, cs], S["factor"][:, cs], ALU.mult),
                      t[bb], rx[bb], S["factor_tok"]) for bb in range(2)]
            if S["both"]:
                squares(S["s2"], xt)
        S["x"][c] = xt
        if S["cA"] is None:
            return
        for _ in range(4):
            if c < 3:
                yield
        for g in range(2):
            bn = 4 + 2 * (c % 2) + g
            bk = bank[bn]

            def f(e, g=g, bk=bk):
                for q in range(4):
                    kt, bb = 4 * c + 2 * g + q // 2, q % 2
                    i = e.transpose(bk[:, q * P:(q + 1) * P], X[:, bb, kt * P:(kt + 1) * P], ident)
                return i
            t = pe(f, xt, bank_free[bn])
            while S["gate"] and (S["gate"], c) not in tk:
                yield
            ts = []
            for q in range(2):
                kt = 4 * c + 2 * g + q
                ts.append(act(lambda e, q=q, kt=kt, bk=bk: e.activation(
                    XT[:, kt, :], bk[:, q * T:(q + 1) * T], ACT.Copy, scale=S["cA"][:, kt:kt + 1]),
                    t, tk[(S["gate"], c)] if S["gate"] else tk["cols"], w))
            bank_free[bn] = ts
            S["xt"][2 * c + g] = ts
            yield

    def turn_rs(S):
        for g in S["bg"]:
            finish(g)
        m, rs = small(2), small(2)
        t = dve(lambda e: e.tensor_reduce(m, S["s1"], AX, ALU.add), S["sq"])
        if not S["both"]:
            return rs, rsqrt_of(m, 2, 1.0 / D, rs, t), None, None
        m2, v, rr = small(2), small(2), small(2)
        t2 = dve(lambda e: e.tensor_reduce(m2, S["s2"], AX, ALU.add), S["sq"])
        t1 = dve(lambda e: e.tensor_scalar(v, m, EPS / D, EPS * EPS, ALU.mult, ALU.add), t)
        t2 = dve(lambda e: e.scalar_tensor_tensor(out=v, in0=m2, scalar=1.0 / D, in1=v, op0=ALU.mult, op1=ALU.add), t1, t2)
        t2 = pool(lambda e: e.tensor_tensor(rr, v, neg_half[:, 0:2], ALU.pow), t2, tk["nh"])
        return rs, rsqrt_of(m, 2, 1.0 / D, rs, t), rr, t2

    def turn_tiles(S, rs, t_rs, cB, b_tok, prefix, then):
        w = S["free"]
        free = E.last("pe")
        t = [dve(lambda e, b=b: e.tensor_scalar(DR[:, b * P:(b + 1) * P], ident, rs[:, b:b + 1], None, ALU.mult), t_rs, w)
             for b in range(2)]
        bk = bank[7]
        t_rb = pe(lambda e: e.matmul(bk[:, 0:T], ones, DR, start=True, stop=True), t, bank_free[7])
        rb = bk[:, 0:T].unsqueeze(1).to_broadcast([P, 2, T])
        tf = [[S[("jk", 0)], S[("jk", 1)]]] * 2
        cut = None
        for g in range(9):
            if g < 8:
                tm = TM[g % 2].rearrange("p (k t) -> p k t", t=T)
                ks = slice(2 * g, 2 * g + 2)
                t = dve(lambda e: e.tensor_tensor(tm, XT[:, ks, :], rb, ALU.mult), t_rb, S["xt"][g], tf[g % 2], w)
                if cB is None:
                    t1 = act(lambda e: e.copy(HTh[:, ks, :], tm), t, free)
                else:
                    t1 = [act(lambda e, q=q: e.activation(HTh[:, 2 * g + q, :], tm[:, q, :], ACT.Identity,
                                                          bias=cB[:, 2 * g + q:2 * g + q + 1]), t, free, b_tok(g // 2)) for q in range(2)]
            if cut:
                k, src, ta, tb = cut
                if cB is None:
                    t2 = dve(lambda e: e.tensor_tensor(HTl[:, k:k + 2, :], src, HTh[:, k:k + 2, :].bitcast(F32), ALU.subtract),
                             tb, ta, free)
                else:
                    t2 = [dve(lambda e, q=q: e.scalar_tensor_tensor(
                        out=HTl[:, k + q, :], in0=src[:, q, :], scalar=cB[:, k + q:k + q + 1],
                        in1=HTh[:, k + q, :].bitcast(F32), op0=ALU.add, op1=ALU.subtract), tb, ta, free, b_tok(k // 4)) for q in range(2)]
                tf[g % 2 - 1] = [tb, t2]
                tk[(prefix, k)] = [tb, t2]
                tk[(prefix, k + 1)] = [tb, t2]
            cut = (2 * g, tm, t, t1)
            bank_free[7] = t
            if g == 8:
                then()
            if g > 3:
                yield

    aTh = over("aTh", 24, 16 * T, FR).rearrange("p (k t) -> p k t", t=T)
    aTl = over("aTl", 40, 16 * T, FR).rearrange("p (k t) -> p k t", t=T)
    SG = [ar(64, 1024).rearrange("p (b n) -> p b n", b=2), ar(68, 1024).rearrange("p (b n) -> p b n", b=2)]
    AN = ar(72, 1024).rearrange("p (b n) -> p b n", b=2)
    FN = ar(16, 2048)

    def gate_out(c):
        def done(b, tok):
            r = [act(lambda e, bb=bb: e.activation(SG[c % 2][:, bb, :], b[bb][:, :], ACT.Silu), tok,
                     tk.get(("sgfree", c % 2)), tk["ffn_mem"]) for bb in range(2)]
            tk[("sg", c)] = r
            return r
        return done

    def up_out(c, k0, free):
        def done(b, tok):
            r = [dve(lambda e, bb=bb: e.tensor_tensor(AN[:, bb, :], b[bb][:, :], SG[c % 2][:, bb, :], ALU.mult),
                     tok, tk[("sg", c)], src_read.get(id(AN)), tk["dg"]) for bb in range(2)]
            tk[("sgfree", c % 2)] = r
            g = to_hl(AN, aTh, aTl, k0, ("ff", c), tk.get(free), r)
            bg.append(g)
            return r
        return done

    VN = ar(16, 8192).rearrange("p (b n) -> p b n", b=2)
    UG = [ar(48, 1024).rearrange("p (b n) -> p b n", b=2), ar(52, 1024).rearrange("p (b n) -> p b n", b=2)]
    GV = [ar(56, 512), ar(58, 512)]
    YN = ar(60, 1024).rearrange("p (b n) -> p b n", b=2)
    SL = ar(64, 1024).rearrange("p (b n) -> p b n", b=2)
    WS = ar(68, 1024).rearrange("p (g n) -> p g n", g=8)
    WT = ar(72, 2048).rearrange("p (b g n) -> p b g n", b=2, g=8)
    FN2 = ar(88, 2048)
    ssv = small(16).rearrange("p (b c) -> p b c", b=2)
    rv_ = small(2)

    def gv_out(c):
        def done(b, tok):
            r, r2 = [], []
            for bb in range(2):
                v = VN[:, bb, 512 * c:512 * c + 512]
                t = act(lambda e, bb=bb, v=v: e.activation(v, b[bb][:, :], ACT.Gelu_apprx_tanh), tok, tk["gmlp_mem"])
                r.append(t)
                r2.append(dve(lambda e, bb=bb, v=v: e.tensor_tensor_reduce(
                    out=b[bb][:, :], in0=v, in1=v, scale=1.0, scalar=0.0, op0=ALU.mult, op1=ALU.add,
                    accum_out=ssv[:, bb, c:c + 1]), t))
            tk[("gv", c)] = r2
            if c == 7:
                bg.append(v_stats())
            return [r, r2]
        return done

    def v_stats():
        s2 = small(2)
        t = dve(lambda e: e.tensor_reduce(s2, ssv, AX, ALU.add), [tk[("gv", c)] for c in range(8)])
        t = rsqrt_of(s2, 2, 1.0 / DI, rv_, t)
        for h in range(2):
            bn = 4 + h
            bk = bank[bn].rearrange("p (h d) -> p h d", d=P)

            def f(e, h=h, bk=bk):
                for i in range(4):
                    i_ = e.transpose(bk[:, i, :], WS[:, 4 * h + i, :], ident)
                return i_
            tp = pe(f, tk["ws"], bank_free[bn])
            r = [dve(lambda e, bb=bb, h=h, bk=bk: e.tensor_scalar(
                WT[:, bb, 4 * h:4 * h + 4, :], bk, rv_[:, bb:bb + 1], None, ALU.mult), tp, t, tk["gmlp_mem"]) for bb in range(2)]
            bank_free[bn] = r
            tk[("wt", h)] = r
            yield

    def u_out(g):
        def done(b, tok):
            r = [act(lambda e, bb=bb: e.activation(UG[g % 2][:, bb, :], b[bb][:, :], ACT.Gelu_apprx_tanh), tok,
                     tk.get(("ugfree", g % 2)), tk["gmlp_mem"]) for bb in range(2)]
            t_g = dma(f"gv{g % 2}", GV[g % 2], a["a_v_gain_2"].rearrange("(a n) -> a n", a=1)[:, 512 * g:512 * g + 512].to_broadcast([P, 512]),
                      tk.get(("gvfree", g % 2)), tk["gmlp_mem"])

            def rest():
                yield
                while ("wt", 1) not in tk:
                    yield
                rr = []
                for bb in range(2):
                    bn = 6 + bb
                    bk = bank[bn]
                    t = pe(lambda e, bb=bb, bk=bk: e.matmul(bk, WT[:, bb, g, :], VN[:, bb, 512 * g:512 * g + 512],
                                                             start=True, stop=True), tk[("wt", g // 4)], tk[("gv", g)], bank_free[bn])
                    v = VN[:, bb, 512 * g:512 * g + 512]
                    t = dve(lambda e, v=v, bk=bk: e.tensor_tensor(v, bk, GV[g % 2], ALU.mult), t, t_g)
                    bank_free[bn] = t
                    u = UG[g % 2][:, bb, :]
                    tk[("gvfree", g % 2)] = t
                    rr.append(dve(lambda e, v=v, u=u: e.scalar_tensor_tensor(
                        out=u, in0=v, scalar=colBS[:, g:g + 1], in1=u, op0=ALU.add, op1=ALU.mult), t, r))
                    yield
                tk[("uy", g)] = rr
            bg.append(rest())
            return r
        return done

    def g2_out(g, k0, free):
        def done(b, tok):
            r, r2 = [], []
            for bb in range(2):
                t = act(lambda e, bb=bb: e.activation(SL[:, bb, :], b[bb][:, :], ACT.Tanh, scale=0.5), tok,
                        tk.get(("slfree", bb)), tk["gmlp_mem"])
                r.append(dve(lambda e, bb=bb: e.scalar_tensor_tensor(
                    out=SL[:, bb, :], in0=SL[:, bb, :], scalar=1.0, in1=b[bb][:, :], op0=ALU.add, op1=ALU.mult), t, tok))
            settle(("uy", g))
            for bb in range(2):
                t = dve(lambda e, bb=bb: e.scalar_tensor_tensor(
                    out=YN[:, bb, :], in0=UG[g % 2][:, bb, :], scalar=0.5, in1=SL[:, bb, :], op0=ALU.mult, op1=ALU.mult),
                    r[bb], tk[("uy", g)], src_read.get(id(YN)), tk["gmlp_mem"])
                tk[("slfree", bb)] = t
                r2.append(t)
            tk[("ugfree", g % 2)] = r2
            bg.append(to_hl(YN, R2h, R2l, k0, ("y", g), tk.get(free), r2))
            return r
        return done

    xm = (HTh, HTl, 0)

    def need_ht(prefix):
        def f(kt):
            settle((prefix, kt))
            return tk[(prefix, kt)]
        return f

    def plain(w, c0, n=512):
        def loads(t0, nkt, dst):
            return [(dst, w.rearrange("(t p) n -> p t n", p=P)[:, t0:t0 + nkt, c0:c0 + n])]
        return loads

    def rowpart(w, r0, c0):
        def loads(t0, nkt, dst):
            return [(dst, w.rearrange("(t p) n -> p t n", p=P)[:, r0 + t0:r0 + t0 + nkt, c0:c0 + 512])]
        return loads

    def ba_loads(t0, nkt, dst):
        w = a["w_in"].rearrange("(t p) n -> p t n", p=P)
        return [(dst[:, :, 0:64], w[:, t0:t0 + nkt, O_KPE:O_KPE + 64]),
                (dst[:, :, 64:80], w[:, t0:t0 + nkt, O_BA:O_BA + 16])]

    def head_loads(w, per, h0, nh, o, n):
        def loads(t0, nkt, dst):
            v = w.rearrange("(t p) (h n) -> p t h n", p=P, n=per)
            return [(dst[:, k, :].rearrange("p (h n) -> p h n", n=n), v[:, t0 + k, h0:h0 + nh, o:o + n]) for k in range(nkt)]
        return loads

    def lat_need(which):
        def f(kt):
            settle(("lat", which, kt))
            return tk[("lat", which, kt)]
        return f

    jobs = []

    def job(*args, **kw):
        jobs.append(Job(*args, **kw))

    win = a["w_in"]
    job("cq", plain(win, O_CQ), 16, 512, xm, "tok", need_ht("ht"), lambda b, t: latent(0, colQA, b, t), lazy=True)
    job("ckv", plain(win, O_CKV), 16, 512, xm, "tok", need_ht("ht"), lambda b, t: latent(1, colKA, b, t), lazy=True)
    job("sm", ba_loads, 16, 80, xm, "tok", need_ht("ht"), small_out, lazy=True)
    for kind, o, c in (("q", O_Q, 0), ("q", O_Q, 1), ("k", O_K, 0)):
        job("g" + kind, plain(win, o + 512 * c), 16, 512, xm, "ch", need_ht("ht"), conv_out(kind, c), lazy=True)
    for c in range(2):
        job("uqn", head_loads(a["w_uq"], 192, 4 * c, 4, 0, P), 4, 512, (R2h, R2l, 0), "ch", lat_need(0), heads_T(qT, 4 * c, ("qT", c)))
    job("uqp", head_loads(a["w_uq"], 192, 0, 8, P, 64), 4, 512, (R2h, R2l, 0), "tok", lat_need(0), q_pe_out, lazy=True)
    for c in range(2):
        job("ukk", head_loads(a["w_ukv"], 256, 4 * c, 4, 0, P), 4, 512, (R2h, R2l, 4), "ch", lat_need(1), heads_T(kT, 4 * c, ("kT", c)))
    for c in range(2):
        job("ukv", head_loads(a["w_ukv"], 256, 4 * c, 4, P, P), 4, 512, (R2h, R2l, 4), "tok", lat_need(1), v_out(c))
    for kind, o, c in (("k", O_K, 1), ("v", O_V, 0), ("v", O_V, 1)):
        job("g" + kind, plain(win, o + 512 * c), 16, 512, xm, "ch", need_ht("ht"), conv_out(kind, c), lazy=True)
    mixer_a = len(jobs)

    def need_omla(kt):
        settle(("omla", kt))
        return tk[("omla", kt)]

    def need_ogdn(kt):
        g = kt // 4
        settle(("ogdn", 1, g))
        return [tk[("ogdn", 0, g)], tk[("ogdn", 1, g)]]
    for c in range(4):
        job("ga", plain(win, O_GATE + 512 * c), 16, 512, xm, "tok", need_ht("ht"), ga_out(c))
        job("om", rowpart(a["w_o_mla"], 0, 512 * c), 8, 512, (R2h, R2l, 0), "tok", need_omla, omla_out(c))
    for c in range(2):
        job("z", plain(win, O_Z + 512 * c), 16, 512, xm, "tok", need_ht("ht"), z_out(c))
    for c in range(4):
        job("gb", plain(win, O_GATE + 2048 + 512 * c), 16, 512, xm, "tok", need_ht("ht"), gb_out(c))
    mixer_b = len(jobs)
    for c in range(4):
        job("og", rowpart(a["w_o_gdn"], 0, 512 * c), 8, 512, (R2h, R2l, 0), "tok", need_ogdn, ogdn_out(c))

    mixer_c = len(jobs)

    def need_mix(kt):
        settle(("mix", kt))
        return tk[("mix", kt)]
    turn2 = new_turn(cAf, "caf", None)
    turn3 = new_turn(colAN, None, FN)
    turn5 = new_turn(None, None, FN2)
    for c in range(4):
        job("wo", plain(a["w_o"], 512 * c), 16, 512, xm, "tok", need_mix, residual(c, "gta", lambda b: ("x2", b), "xa", turn2))
    mixer_d = len(jobs)

    parts = [(0, 4), (4, 8), (8, 11)]
    for n, (c0, c1) in enumerate(parts):
        for c in range(c0, c1):
            if c == 0 or c > c0:
                job("gate", plain(a["w_gate_up"], 512 * c), 16, 512, xm, "tok", need_ht("h2"), gate_out(c))
            job("up", plain(a["w_gate_up"], FF + 512 * c), 16, 512, xm, "tok", need_ht("h2"), up_out(c, 4 * (c - c0), ("at", n - 1)))
        if n < 2:
            job("gate", plain(a["w_gate_up"], 512 * c1), 16, 512, xm, "tok", need_ht("h2"), gate_out(c1))
        for c in range(4):
            def need_ff(kt, c0=c0):
                key = (("ff", c0 + kt // 4), kt)
                settle(key)
                return tk[key]
            res = residual(c, "gtf", lambda b: ("x2", b), "xb", turn3 if n == 2 else None)

            def fin(b, tok, c=c, n=n, res=res):
                r = res(b, tok)
                if c == 3:
                    tk[("at", n)] = tok
                return r
            job("down", rowpart(a["w_down"], 4 * c0, 512 * c), 4 * (c1 - c0), 512, (aTh, aTl, 0), "tok", need_ff, fin)
    ffn_end = len(jobs)

    w2 = a["a_w_in_2"]
    for c in range(8):
        job("v2", plain(w2, DI + 512 * c), 16, 512, xm, "tok", need_ht("h3"), gv_out(c))
    for n in range(4):
        for g in (2 * n, 2 * n + 1):
            if g == 0 or g % 2:
                job("u2", plain(w2, 512 * g), 16, 512, xm, "tok", need_ht("h3"), u_out(g))
            job("g2", plain(w2, 2 * DI + 512 * g), 16, 512, xm, "tok", need_ht("h3"), g2_out(g, 4 * (g % 2), ("yt", n - 1)))
        if n < 3:
            job("u2", plain(w2, 512 * (2 * n + 2)), 16, 512, xm, "tok", need_ht("h3"), u_out(2 * n + 2))
        for c in range(4):
            def need_y(kt, n=n):
                key = (("y", 2 * n + kt // 4), kt)
                settle(key)
                return tk[key]
            res = residual(c, None, lambda b: ("x3", b), "xc", turn5 if n == 3 else None)

            def fin(b, tok, c=c, n=n, res=res):
                r = res(b, tok)
                if c == 3:
                    tk[("yt", n)] = tok
                return r
            job("wout", rowpart(a["a_w_out_2"], 8 * n, 512 * c), 8, 512, (R2h, R2l, 0), "tok", need_y, fin)

    def ada(sections):
        return [("g", s + 512 * c, q) for c in range(4) for s in sections for q in range(4)]
    later = ada([8192, 6144]) + ada([4096]) + ada([10240])
    plan(jobs, later, 2)

    start_loads()
    for _ in range(4):
        stage_next()
    columns()
    for _ in range(2):
        stage_next()
    rs1 = small(2)
    XS1 = ar(16, 4096).rearrange("p (b n) -> p b n", b=2)
    tmp1 = [ar(32, 512), ar(34, 512)]
    tx = [tk[("x", 0)], tk[("x", 1)]]
    t_rs = row_scale(X, XS1, rs1, tx)
    bg.append(mod_scale(cAm, colNM, 16, "cam"))
    bg.append(transposed(X, rs1, XS1, cAm, cBm, tmp1, lambda kt: [("cam", kt // 4), ("mod", 4 * (kt // 4))], "ht",
                         None, [6, 7], t_rs, tx))
    slot()
    rope_tables()
    group = [(jobs[0], (bank[0], bank[1])), (jobs[1], (bank[2], bank[3])), (jobs[2], (bank[4][:, 0:80], bank[4][:, 80:160]))]
    last = {}
    for c in range(4):
        while units[staged[0]][0] == "g" and len(halves) == used[0]:
            stage_next()
            slot()
        for n, (j, b) in enumerate(group):
            for _ in range(2):
                last[n] = consume(j, b, tk["cols"], n == 2)[1]
                slot()
    settle(("ht", 15))
    tk["ht_done"] = [E.last("pe"), E.last("act"), E.last("dve")]
    tk["raw1"] = raw_free[NR:]
    for n in range(2):
        cv_free[n] = tk[("sq", n)] = tk["raw1"]
    ct_free[0] = tk["raw1"]
    bg.append(mod_scale(cAf, colNF, 64, "caf"))
    bg.append(attention())
    retire(jobs[0], group[0][1], last[0], 0)
    retire(jobs[1], group[1][1], last[1], 1)

    def sm_whole():
        bank_free[4] = last[2]
        bank_free[4] = yield from jobs[2].done(group[2][1], last[2])
        tk["sm"] = bank_free[4]
    bg.append(sm_whole())
    current[0] = 1
    turns = {"uqn": [False, True], "ukk": [False, True]}
    for j in jobs[3:mixer_a]:
        run(j, j.name in turns and turns[j.name].pop(0))

    def cells():
        for k in ["attention", "gate"] + [("nat", x, h) for x in "qkv" for h in range(2)]:
            while k not in tk:
                yield
        bg.append(cell(0, 0))
        bg.append(cell(0, 1))
        bg.append(gdn_final())
    bg.append(cells())
    for j in jobs[mixer_a:mixer_b]:
        run(j)
    settle(("ogdn", 1, 1))
    for b in range(2):
        tk[("x2", b)] = dma(f"x{b}", X[:, b, :], a["x"][b * P:(b + 1) * P, :], tk["o_read"], tk[("cell", 1, 0)], tk[("cell", 1, 1)])
    bg.append(spread(colGA, 32, "gta", tk["o_read"], tk[("ogdn", 1, 1)], tk[("cell", 1, 0)], tk[("cell", 1, 1)]))
    for j in jobs[mixer_b:mixer_c]:
        run(j)
    turn2["free"] = [E.last("pe"), E.last("act"), E.last("dve")]
    for j in jobs[mixer_c:mixer_d]:
        run(j)
    settle(("gta", 3))

    t_all = [E.last("pe"), E.last("act"), E.last("dve")]
    tk["ffn_mem"] = t_all
    tk_fn = dma("fn", FN, a["final_norm"].rearrange("(a n) -> a n", a=1).to_broadcast([P, D]), t_all)
    rs, t_rs, _, _ = turn_rs(turn2)
    for q in range(4):
        settle(("mod", 48 + 4 * q))

    def after_h2():
        tk["ffn_mem"] = [E.last("act"), E.last("dve"), E.last("pe")]
        bg.append(spread(colGF, 80, "gtf", tk["ffn_mem"]))
    bg.append(turn_tiles(turn2, rs, t_rs, cBf, lambda q: tk[("mod", 48 + 4 * q)], "h2", after_h2))
    slot()
    for j in jobs[mixer_d:ffn_end - 4]:
        run(j)
    turn3["free"] = [E.last("pe"), E.last("act"), E.last("dve")]
    turn3["factor_tok"] = tk_fn
    for j in jobs[ffn_end - 4:ffn_end]:
        run(j)

    rs3, t_rs3, rr, t_rr = turn_rs(turn3)

    def after_h3():
        for b in range(2):
            tk[("x3", b)] = dve(lambda e, b=b: e.tensor_scalar(X[:, b, :], X[:, b, :], rs3[:, b:b + 1], None, ALU.mult),
                                t_rs3, [turn3["x"][c] for c in range(4)], turn3["pe"])
        tk["gmlp_mem"] = [E.last("act"), E.last("dve"), E.last("pe")]
        tk["ws"] = dma("ws", WS, a["a_w_s_2"].rearrange("g p q -> p g q"), tk["gmlp_mem"])
        tk["fn2"] = dma("fn", FN2, a["final_norm_2"].rearrange("(a n) -> a n", a=1).to_broadcast([P, D]), tk["gmlp_mem"])
    turn3["pe"] = E.last("pe")
    bg.append(turn_tiles(turn3, rr, t_rr, None, None, "h3", after_h3))
    slot()
    for j in jobs[ffn_end:-4]:
        run(j)
    turn5["free"] = [E.last("pe"), E.last("act"), E.last("dve")]
    turn5["factor_tok"] = tk["fn2"]
    for j in jobs[-4:]:
        run(j)

    rs, t_rs, _, _ = turn_rs(turn5)
    for h in range(2):
        hs = slice(1024 * h, 1024 * h + 1024)
        for b in range(2):
            if b == 0:
                t = dve(lambda e: e.tensor_scalar(X[:, 0, hs], X[:, 0, hs], rs[:, 0:1], None, ALU.mult), t_rs, [turn5["x"][c] for c in range(4)])
            else:
                t = act(lambda e: e.activation(X[:, 1, hs], X[:, 1, hs], ACT.Copy, scale=rs[:, 1:2]), t_rs, [turn5["x"][c] for c in range(4)])
            t_out = dma("out", out[b * P:(b + 1) * P, hs], X[:, b, hs], t)
    E.waits("sp", [t_out])


_LAYER = ("w_ada", "b_ada", "norm_mix", "norm_ffn", "w_in", "q_a_norm", "kv_a_norm", "w_uq", "w_ukv", "w_o_mla",
          "conv_w", "A_log", "dt_bias", "gdn_norm", "w_o_gdn", "w_o", "w_gate_up", "w_down",
          "a_norm_2", "a_w_in_2", "a_v_gain_2", "a_w_s_2", "a_b_s_2", "a_w_out_2")
_WHOLE = ("c", "positions", "final_norm", "final_norm_2")


def kernel(**inputs):
    import concourse.bacc as _bacc
    from concourse.bass_utils import run_bass_kernel_spmd as _run

    nc = _bacc.Bacc("TRN2", target_bir_lowering=False, num_devices=1, dynamic_dma_scratch_size=1024)
    host = {"x": np.asarray(inputs["x"])[0], "cst": shape_constants()}
    for name in _LAYER:
        host[name] = np.asarray(inputs[name])[0]
    for name in _WHOLE:
        host[name] = np.asarray(inputs[name])
    arrays, views = {}, {}
    for name, v in host.items():
        v = np.ascontiguousarray(v)
        key = f"in_{name}_dram"
        arrays[key] = v
        views[name] = nc.dram_tensor(key, v.shape, mybir.dt.from_np(v.dtype), kind="ExternalInput").ap()
    out = nc.dram_tensor("out_dram", (T, D), F32, kind="ExternalOutput").ap()
    program(nc, views, out)
    r = _run(nc, [arrays], core_ids=[0])
    return np.asarray(r.results[0]["out_dram"]).reshape(1, T, D)
```
